# Optimizing a Trainium2 kernel written in Bass

```python
import jax, jax.numpy as jnp
from jax import lax
import numpy as np

D_MODEL = 2048
BATCH = 1
SEQ = 512
DEPTH = 1

D_CONV = D_MODEL // 2
CONV_WIDTH = 31
D_POOL = D_MODEL // 2
POOL_WINDOWS = (2, 4, 8, 16)
N_POOL_GROUPS = len(POOL_WINDOWS)
POOL_GROUP_DIM = D_POOL // N_POOL_GROUPS
N_BRANCHES = 2
D_IN_PROJ = 2 * D_CONV + D_POOL + N_BRANCHES * D_MODEL
D_FF = 5632
FFN_CONV_WIDTH = 3
PLE_DIM = 256
EPS = 1e-6

kernel_name = "hybrid_conformer_pool_gated_block"

def rmsnorm(x, g):
    xf = x.astype(jnp.float32)
    y = xf * lax.rsqrt(jnp.mean(xf * xf, axis=-1, keepdims=True) + EPS) * g.astype(jnp.float32)
    return y.astype(x.dtype)

def layernorm(x, g, b):
    xf = x.astype(jnp.float32)
    mu = jnp.mean(xf, axis=-1, keepdims=True)
    var = jnp.mean(jnp.square(xf - mu), axis=-1, keepdims=True)
    y = (xf - mu) * lax.rsqrt(var + EPS) * g.astype(jnp.float32) + b.astype(jnp.float32)
    return y.astype(x.dtype)

def causal_depthwise_conv(u, w, b):
    k, c = w.shape
    y = lax.conv_general_dilated(
        u, w[:, None, :].astype(u.dtype),
        window_strides=(1,), padding=[(k - 1, 0)],
        dimension_numbers=("NWC", "WIO", "NWC"),
        feature_group_count=c)
    return y + b.astype(u.dtype)

def causal_pool_minus_self(u, window):
    uf = u.astype(jnp.float32)
    seq = uf.shape[1]
    cs = jnp.cumsum(uf, axis=1)
    shifted = jnp.pad(cs[:, :-window], ((0, 0), (window, 0), (0, 0)))
    count = jnp.minimum(jnp.arange(seq, dtype=jnp.float32) + 1.0, float(window))
    mean = (cs - shifted) / count[None, :, None]
    return (mean - uf).astype(u.dtype)

def setup_inputs(seed: int = 0) -> dict:
    key = jax.random.key(seed)
    ks = jax.random.split(key, 32)
    nrm = lambda k, shape, scale: jax.random.normal(k, shape, jnp.float32) * scale
    gain = lambda k, n: 1.0 + 0.01 * jax.random.normal(k, (n,), jnp.float32)
    return {
        "x": nrm(ks[0], (BATCH, SEQ, D_MODEL), 1.0),
        "p": nrm(ks[1], (DEPTH, BATCH, SEQ, PLE_DIM), 1.0),
        "mix_pre_g": gain(ks[2], D_MODEL),
        "w_in": nrm(ks[3], (D_MODEL, D_IN_PROJ), D_MODEL ** -0.5),
        "conv_a_w": nrm(ks[4], (CONV_WIDTH, D_CONV), CONV_WIDTH ** -0.5),
        "conv_a_b": nrm(ks[5], (D_CONV,), 0.01),
        "ln_a_g": gain(ks[6], D_CONV),
        "ln_a_b": nrm(ks[7], (D_CONV,), 0.01),
        "w_a_out": nrm(ks[8], (D_CONV, D_MODEL), D_CONV ** -0.5),
        "pool_w": nrm(ks[9], (N_POOL_GROUPS, POOL_GROUP_DIM, POOL_GROUP_DIM), POOL_GROUP_DIM ** -0.5),
        "pool_scale": 1.0 + 0.1 * jax.random.normal(ks[10], (D_POOL,), jnp.float32),
        "w_b_out": nrm(ks[11], (D_POOL, D_MODEL), D_POOL ** -0.5),
        "w_o": nrm(ks[12], (D_MODEL, D_MODEL), D_MODEL ** -0.5),
        "mix_post_g": gain(ks[13], D_MODEL),
        "ffn_pre_g": gain(ks[14], D_MODEL),
        "w_up": nrm(ks[15], (D_MODEL, 2 * D_FF), D_MODEL ** -0.5),
        "conv_f_w": nrm(ks[16], (FFN_CONV_WIDTH, 2 * D_FF), FFN_CONV_WIDTH ** -0.5),
        "conv_f_b": nrm(ks[17], (2 * D_FF,), 0.01),
        "w_down": nrm(ks[18], (D_FF, D_MODEL), D_FF ** -0.5),
        "ffn_post_g": gain(ks[19], D_MODEL),
        "w_ple": nrm(ks[20], (PLE_DIM, D_MODEL), PLE_DIM ** -0.5),
        "w_ple_gate": nrm(ks[21], (D_MODEL, D_MODEL), D_MODEL ** -0.5),
        "ple_post_g": gain(ks[22], D_MODEL),
    }

def reference(x, p, mix_pre_g, w_in, conv_a_w, conv_a_b, ln_a_g, ln_a_b, w_a_out,
              pool_w, pool_scale, w_b_out, w_o, mix_post_g, ffn_pre_g, w_up,
              conv_f_w, conv_f_b, w_down, ffn_post_g, w_ple, w_ple_gate, ple_post_g):
    bsz, seq, _ = x.shape
    for i in range(DEPTH):
        h = rmsnorm(x, mix_pre_g)
        proj = h @ w_in
        a_in, b_in, gates = jnp.split(proj, [2 * D_CONV, 2 * D_CONV + D_POOL], axis=-1)

        a_val, a_gate = jnp.split(a_in, 2, axis=-1)
        a = a_val * jax.nn.sigmoid(a_gate)
        a = causal_depthwise_conv(a, conv_a_w, conv_a_b)
        a = jax.nn.silu(layernorm(a, ln_a_g, ln_a_b))
        y_a = a @ w_a_out

        b_groups = b_in.reshape(bsz, seq, N_POOL_GROUPS, POOL_GROUP_DIM)
        pooled = jnp.stack(
            [causal_pool_minus_self(b_groups[:, :, g], w) for g, w in enumerate(POOL_WINDOWS)],
            axis=2)
        mixed = jnp.einsum("bsgc,gcd->bsgd", pooled, pool_w).reshape(bsz, seq, D_POOL)
        y_b = (mixed * pool_scale) @ w_b_out

        g_a, g_b = jnp.split(jax.nn.sigmoid(gates), N_BRANCHES, axis=-1)
        merged = g_a * y_a + g_b * y_b
        x = x + rmsnorm(merged @ w_o, mix_post_g)

        h2 = rmsnorm(x, ffn_pre_g)
        up = causal_depthwise_conv(h2 @ w_up, conv_f_w, conv_f_b)
        u_gate, u_val = jnp.split(up, 2, axis=-1)
        f = (jax.nn.gelu(u_gate, approximate=True) * u_val) @ w_down
        x = x + rmsnorm(f, ffn_post_g)

        e = (p[i] @ w_ple) * jax.nn.sigmoid(x @ w_ple_gate)
        x = x + rmsnorm(e, ple_post_g)
    return x


_drawn_inputs = setup_inputs


def setup_inputs(seed=0):
    import zlib

    import numpy as np

    out = dict(_drawn_inputs(seed))
    spreads = {}
    factors = {'mix_pre_g': 6.708,
     'conv_a_b': 23.226,
     'ln_a_g': 46.657,
     'ln_a_b': 49.544,
     'mix_post_g': 30.668,
     'ffn_pre_g': 36.441,
     'conv_f_b': 37.076,
     'ffn_post_g': 173.955,
     'ple_post_g': 200.0}
    for name, (base, spread) in spreads.items():
        noise = np.random.default_rng([zlib.crc32(name.encode()), seed]).standard_normal(out[name].shape)
        drawn = base * np.exp(spread * noise) if base else spread * noise
        out[name] = __import__('jax').numpy.asarray(drawn.astype(out[name].dtype))
    for name, factor in factors.items():
        out[name] = (out[name] * factor).astype(out[name].dtype)
    return out
```

```python
from contextlib import ExitStack

import numpy as np

import concourse.bass as bass
from concourse import mybir

F32 = mybir.dt.float32
F32R = mybir.dt.float32r
ALU = mybir.AluOpType
ACT = mybir.ActivationFunctionType

P = 128
TOK = 512
BLK = TOK // P
D = 2048
DC = D // P
H = D // 2
HC = H // P
FF = 5632
FC = FF // P
CONV_W = 31
PAD = CONV_W - 1
WINDOWS = (2, 4, 8, 16)
PGD = H // len(WINDOWS)
PPAD = 16
FTAPS = 3
PLE = 256
PLEC = PLE // P
EPS = 1e-6
GRP = 4
NGRP = FC // GRP

UNIT = 8 * P
RAW, SLOTS, BANKS = 2, 4, 4

U_B = 0
U_P = U_B + 2 * HC
U_A = U_P + 2
U_M1 = U_A + 4 * HC
U_M2 = U_M1 + 3 * DC
U_O = U_M2 + 3 * DC
U_F = U_O + 2 * DC
U_L = U_F + 4 * FC + 8 * NGRP
U_G = U_L + 4
U_END = U_G + 2 * DC
T_B = DC
T_P = T_B + HC
T_A = T_P + HC
T_M1 = T_A + 2 * HC
T_M2 = T_M1 + 2 * DC
T_O = T_M2 + 2 * DC
T_F = T_O + DC
T_G = T_F + 2 * FC + DC * NGRP
Q_LN, Q_O, Q_X2, Q_F, Q_E = 0, HC, HC + DC, HC + 2 * DC, HC + 3 * DC
S_LN, S_X2, S_F, S_E = 0, HC, HC + DC, HC + 2 * DC
G_A, G_M1, G_M2, G_G = 0, HC, HC + DC, HC + 2 * DC

C_MIXPRE, C_MIXPOST, C_FFNPRE, C_FFNPOST, C_PLEPOST = 0, DC, 2 * DC, 3 * DC, 4 * DC
C_CAB = 5 * DC
C_LNG = C_CAB + HC
C_LNB = C_LNG + HC
C_PSC = C_LNB + HC
C_CAW = C_PSC + HC
C_CFB = C_CAW + CONV_W * HC
C_CFW = C_CFB + 2 * FC
C_ALL = C_CFW + FTAPS * 2 * FC


class At:

    def __init__(self, c, i=None, k=0):
        self.c, self.i, self.k = c, i, k

    def __add__(self, n):
        return At(self.c + n, self.i, self.k)

    def value(self):
        return self.c if self.i is None or self.k == 0 else self.i * self.k + self.c

    def slot(self, n):
        assert self.k % n == 0
        return self.c % n

    def raw_count(self):
        assert self.k % RAW == 0
        return At(16 * (self.c // RAW + 1), self.i, 16 * self.k // RAW)


class Tally:

    def __init__(self, eng, sem):
        self.eng, self.sem, self.at = eng, sem, At(0)

    def __call__(self, ins):
        ins.then_inc(self.sem, 1)
        self.at = self.at + 1

    def settle(self):
        self.eng.wait_ge(self.sem, self.at.value())

    def enter(self, i, per):
        self.base, self.at = self.at.c, At(self.at.c, i, per)

    def leave(self, n, per):
        assert self.at.c - self.base == per, f"the loop adds {self.at.c - self.base}, not {per}"
        self.at = At(self.base + n * per)


def build(nc, x, p, mix_pre_g, w_in, conv_a_w, conv_a_b, ln_a_g, ln_a_b, w_a_out, pool_w, pool_scale, w_b_out,
          w_o, mix_post_g, ffn_pre_g, w_up, conv_f_w, conv_f_b, w_down, ffn_post_g, w_ple, w_ple_gate,
          ple_post_g, out):
    xt_dram = nc.dram_tensor("xt_dram", (P, DC, TOK), F32, kind="Internal").ap()
    x2_dram = nc.dram_tensor("x2_dram", (P, DC, TOK), F32, kind="Internal").ap()
    ctx = ExitStack()
    with ctx:
        sem = lambda name: ctx.enter_context(nc.semaphore(name))

        cursor = [16512]

        def region(nbytes):
            at = cursor[0]
            cursor[0] += (nbytes + 63) // 64 * 64
            return at

        def place(name, shape, dt, offset):
            return nc.alloc_sbuf_tensor_at(name, shape, dt, offset=offset)

        FULL = DC * TOK * 4
        r_raw, r_whi, r_wlo = region(RAW * UNIT * 4), region(SLOTS * UNIT * 4), region(SLOTS * UNIT * 4)
        r1, r2, r3, r4 = region(FULL), region(FULL), region(FULL), region(FULL)
        r5 = region(HC * (PAD + TOK) * 4)
        w_raw = place("w_raw", [P, RAW, UNIT], F32, r_raw)
        w_hi = place("w_hi", [P, SLOTS, UNIT], F32R, r_whi)
        w_lo = place("w_lo", [P, SLOTS, UNIT], F32R, r_wlo)
        xg_hi = place("xg_hi", [P, DC, TOK], F32R, r1)
        xg_lo = place("xg_lo", [P, DC, TOK], F32R, r2)
        x2_back = place("x2_back", [P, DC, TOK], F32, r1)
        x3_hi = place("x3_hi", [P, DC, TOK], F32R, r2)
        y_nat = place("y_nat", [P, 2, BLK, TOK], F32, r2)
        xt = place("xt", [P, DC, TOK], F32, r3)
        pooled_hi = place("pooled_hi", [P, HC, TOK], F32R, r3)
        pooled_lo = place("pooled_lo", [P, HC, TOK], F32R, r3 + FULL // 2)
        merged = place("merged", [P, DC, TOK], F32, r3)
        x2 = place("x2", [P, DC, TOK], F32, r3)
        f_acc = place("f_acc", [P, DC, TOK], F32, r3)
        x3_lo = place("x3_lo", [P, DC, TOK], F32R, r3)
        x_nat = place("x_nat", [P, BLK, D], F32, r4)
        mixed_hi = place("mixed_hi", [P, HC, TOK], F32R, r4)
        mixed_lo = place("mixed_lo", [P, HC, TOK], F32R, r4 + FULL // 2)
        a_hi = place("a_hi", [P, HC, TOK], F32R, r4)
        a_lo = place("a_lo", [P, HC, TOK], F32R, r4 + FULL // 2)
        og = place("og", [P, DC, TOK], F32, r4)
        g_hi = place("g_hi", [P, 2, GRP, TOK], F32R, r4)
        g_lo = place("g_lo", [P, 2, GRP, TOK], F32R, r4 + FULL // 2)
        e_buf = place("e_buf", [P, DC, TOK], F32, r4)
        par_nat = place("par_nat", [P, 7, P], F32, r5)
        u_pool = place("u_pool", [P, PPAD + TOK], F32, r5 + 4096)
        s_pool = place("s_pool", [P, 2, PPAD + TOK], F32, r5 + 6400)
        pool_f = place("pool_f", [P, TOK], F32, r5 + 10752)
        a_conv = place("a_conv", [P, HC, PAD + TOK], F32, r5)
        up_gate = place("up_gate", [P, 2 + TOK], F32, r5)
        up_val = place("up_val", [P, 2 + TOK], F32, r5 + 2112)
        gate_c = place("gate_c", [P, TOK], F32, r5 + 4224)
        val_c = place("val_c", [P, TOK], F32, r5 + 6272)
        gelu_g = place("gelu_g", [P, TOK], F32, r5 + 8320)
        ff_prod = place("ff_prod", [P, TOK], F32, r5 + 10368)
        p_nat = place("p_nat", [P, BLK, PLE], F32, r5)
        p_hi = place("p_hi", [P, PLEC, TOK], F32R, r5 + 4096)
        p_lo = place("p_lo", [P, PLEC, TOK], F32R, r5 + 8192)
        small = lambda name, shape: place(name, shape, F32, region(4 * int(np.prod(shape[1:]))))
        par = small("par", [P, C_ALL])
        ident = small("ident", [P, P])
        ones = small("ones", [P, P])
        diag = small("diag", [P, BLK, P])
        r_bc = small("r_bc", [P, TOK])
        sq = small("sq", [P, 2, TOK])
        acc = small("acc", [P, TOK])
        scaled = small("scaled", [P, TOK])
        sig = small("sig", [P, TOK])
        tmp = small("tmp", [P, TOK])
        conv_acc = small("conv_acc", [P, TOK])
        x_sums = small("x_sums", [P, 2 * BLK])
        x_sum = small("x_sum", [P, BLK])
        std = small("std", [P, BLK])
        rstd = small("rstd", [P, BLK])
        eps = small("eps", [P, 1])
        inv_count = small("inv_count", [P, PPAD])
        assert cursor[0] <= nc.sbuf_usable_end, cursor[0]
        ps = ctx.enter_context(nc.psum_tensor("ps", [P, 8, TOK], F32))
        B_SUM, B_PAR, B_PAR2, B_BC = 4, 5, 6, 7

        raw_in = [sem(f"raw_in{s}") for s in range(RAW)]
        slots_freed = sem("slots_freed")
        hi_ready, lo_ready, units_done = sem("hi_ready"), sem("lo_ready"), sem("units_done")
        tiles_taken, dve_chain = sem("tiles_taken"), sem("dve_chain")
        x_in = [sem("x_in0"), sem("x_in1")]
        par_in0, par_in1 = sem("par_in0"), sem("par_in1")
        consts_ready, ident_zero = sem("consts_ready"), sem("ident_zero")
        par_turned, par_ready, x_turned = sem("par_turned"), sem("par_ready"), sem("x_turned")
        xg_hi_ready, xg_ready, x_squares = sem("xg_hi_ready"), sem("xg_ready"), sem("x_squares")
        x_sums_ready, mean_sum_ready = sem("x_sums_ready"), sem("mean_sum_ready")
        sums_done, std_ready = sem("sums_done"), sem("std_ready")
        diag_ready, spread_done = sem("diag_ready"), sem("spread_done")
        pool_f_ready, pooled_hi_ready, pooled_ready = sem("pool_f_ready"), sem("pooled_hi_ready"), sem("pooled_ready")
        mixed_hi_ready, sigmoid_ready = sem("mixed_hi_ready"), sem("sigmoid_ready")
        centred, squares_ready, squares_added = sem("centred"), sem("squares_ready"), sem("squares_added")
        ln_scaled, silu_ready, a_hi_ready, a_ready = (sem(n) for n in ("ln_scaled", "silu_ready", "a_hi_ready", "a_ready"))
        merged_ready, merged_hi_ready, merged_split = (sem(n) for n in ("merged_ready", "merged_hi_ready", "merged_split"))
        x2_ready, x2g_hi_ready, x2g_ready = sem("x2_ready"), sem("x2g_hi_ready"), sem("x2g_ready")
        first_tap_ready, gate_conv_ready, gelu_ready = (sem(n) for n in ("first_tap_ready", "gate_conv_ready", "gelu_ready"))
        ff_ready, g_hi_ready, g_ready = sem("ff_ready"), sem("g_hi_ready"), sem("g_ready")
        x3_ready, x3_hi_ready, x3_split = sem("x3_ready"), sem("x3_hi_ready"), sem("x3_split")
        ple_taken = sem("ple_taken")
        y_ready, y_turned, y_taken = sem("y_ready"), sem("y_turned"), sem("y_taken")
        xt_out, xt_in, x2_out, f_zero, x2_in = (sem(n) for n in ("xt_out", "xt_in", "x2_out", "f_zero", "x2_in"))
        p_in, p_turned, p_hi_ready, p_ready = sem("p_in"), sem("p_turned"), sem("p_hi_ready"), sem("p_ready")
        out_done = [sem("out_done0"), sem("out_done1")]

        block = ctx.enter_context(nc.Block())
        F_UP = lambda j: U_F if j == 0 else U_F + 4 * GRP + 24 * (j - 1)
        F_DOWN = lambda j: U_F + 4 * GRP + 24 * j + (4 * GRP if j < NGRP - 1 else 0)
        FT_UP = lambda j: T_F if j == 0 else T_F + 2 * GRP + 24 * (j - 1)
        FT_DOWN = lambda j: T_F + 2 * GRP + 24 * j + (2 * GRP if j < NGRP - 1 else 0)

        @block.sync
        def _(sp):
            for_k = lambda w: w.rearrange("(k p) n -> p k n", p=P)
            win, wa, wb, wo = for_k(w_in), for_k(w_a_out), for_k(w_b_out), for_k(w_o)
            wup, wdn, wpg, wpl = for_k(w_up), for_k(w_down), for_k(w_ple_gate), for_k(w_ple)

            def load(u, src, width=P):
                if not (u.i is None and u.c < RAW):
                    sp.wait_ge(lo_ready, (u + (1 - RAW)).value())
                    sp.sem_inc(slots_freed, 1)
                s = u.slot(RAW)
                sp.dma_start(w_raw[:, s].rearrange("p (k n) -> p k n", n=width), src).then_inc(raw_in[s], 16)

            def column(u, w, col, halves=2):
                for h in range(halves):
                    load(u + h, w[:, 8 * h:8 * h + 8, bass.ds(col, P)])

            for h in range(2):
                for b in range(BLK):
                    sp.dma_start(x_nat[:, b, h * H:(h + 1) * H], x[0, b * P:(b + 1) * P, h * H:(h + 1) * H]).then_inc(x_in[h], 16)
                if h == 0:
                    column(At(U_B), win, 2 * H)
            with sp.Fori(1, HC) as c:
                column(At(U_B, c, 2), win, c * P + 2 * H)
            pw = pool_w.rearrange("g (k p) d -> p (g k) d", p=P)
            for n in range(2):
                load(At(U_P + n), pw[:, 4 * n:4 * n + 4, :], PGD)
            with sp.Fori(0, HC) as c:
                column(At(U_A, c, 4), win, c * P + H)
                column(At(U_A + 2, c, 4), win, c * P)
            for first, w, gates in ((U_M1, wb, 3 * H + D), (U_M2, wa, 3 * H)):
                with sp.Fori(0, DC // 2) as m2:
                    for j in range(2):
                        column(At(first + 3 * j, m2, 6), win, m2 * (2 * P) + (gates + j * P))
                        column(At(first + 3 * j + 2, m2, 6), w, m2 * (2 * P) + j * P, halves=1)
            with sp.Fori(0, DC) as m:
                column(At(U_O, m, 2), wo, m * P)

            def down(u, row, v):
                load(u, wdn[:, row:row + GRP, bass.ds(v, 2 * P)] if isinstance(row, int) else wdn[:, bass.ds(row, GRP), v:v + 2 * P], 2 * P)

            with sp.Fori(0, GRP) as c:
                column(At(F_UP(0), c, 4), wup, c * P)
                column(At(F_UP(0) + 2, c, 4), wup, c * P + FF)
            with sp.Fori(0, NGRP - 1) as j:
                for c in range(GRP):
                    column(At(F_UP(1) + 4 * c, j, 24), wup, j * (GRP * P) + (GRP + c) * P)
                    column(At(F_UP(1) + 4 * c + 2, j, 24), wup, j * (GRP * P) + ((GRP + c) * P + FF))
                for v in range(DC // 2):
                    down(At(F_DOWN(0) + v, j, 24), j * GRP, v * 2 * P)
            with sp.Fori(0, DC // 4) as v2:
                for k in range(2):
                    down(At(F_DOWN(NGRP - 1) + k, v2, 2), (NGRP - 1) * GRP, v2 * (4 * P) + k * 2 * P)
            for n in range(4):
                load(At(U_L + n), wpl[:, :, n * TOK:(n + 1) * TOK], TOK)
            with sp.Fori(0, DC) as m:
                column(At(U_G, m, 2), wpg, m * P)
            rows = out.rearrange("a (b t) d -> t (a b) d", t=P)
            for q in range(DC // 4):
                sp.wait_ge(y_taken, BLK * (q + 1))
                sp.dma_start(rows[:, :, q * TOK:(q + 1) * TOK], y_nat[:, q % 2]).then_inc(out_done[q % 2], 16)
            for s in range(2):
                sp.wait_ge(out_done[s], 32)

        @block.gpsimd
        def _(pool):
            nc.gpsimd.memset(ident[:], 0.0).then_inc(ident_zero, 1)
            pool.wait_ge(ident_zero, 1)
            nc.gpsimd.affine_select(out=ident[:], in_=ident[:], compare_op=ALU.not_equal, fill=1.0, base=0,
                                    pattern=[[-1, P]], channel_multiplier=1).then_inc(consts_ready, 1)
            nc.gpsimd.memset(ones[:], 1.0).then_inc(consts_ready, 1)
            nc.gpsimd.memset(eps[:], EPS).then_inc(consts_ready, 1)
            for t in range(PPAD):
                nc.gpsimd.memset(inv_count[:, t:t + 1], 1.0 / (t + 1)).then_inc(consts_ready, 1)
            pool.wait_ge(tiles_taken, DC)
            pool.dma_start(xt_dram, xt[:]).then_inc(xt_out, 16)
            pool.wait_ge(xt_out, 16)
            pool.wait_ge(merged_split, DC)
            pool.dma_start(xt[:], xt_dram).then_inc(xt_in, 16)
            pool.wait_ge(x2_ready, DC)
            pool.wait_ge(x2g_ready, DC)
            pool.dma_start(x2_dram, x2[:]).then_inc(x2_out, 16)
            pool.wait_ge(x2_out, 16)
            pool.wait_ge(squares_ready, Q_X2 + DC)
            nc.gpsimd.memset(f_acc[:], 0.0).then_inc(f_zero, 1)
            pool.wait_ge(units_done, F_UP(NGRP - 1) + 4 * GRP)
            pool.dma_start(x2_back[:], x2_dram).then_inc(x2_in, 16)
            pool.wait_ge(g_ready, FC)
            pool.dma_start(p_nat[:], p.rearrange("z a (b t) d -> t (z a b) d", t=P)).then_inc(p_in, 16)

        @block.tensor
        def _(pe):
            pe.wait_ge(consts_ready, 2)

            def bank_free(t):
                if not (t.i is None and t.c < BANKS):
                    pe.wait_ge(tiles_taken, (t + (1 - BANKS)).value())

            def products(o, s, cols, hi, lo, start, stop):
                pe.matmul(o, w_hi[:, s, cols], hi, start=start, stop=False)
                pe.matmul(o, w_hi[:, s, cols], lo, start=False, stop=False)
                return pe.matmul(o, w_lo[:, s, cols], hi, start=False, stop=stop)

            def tile(u, t, hi, lo, chunks=DC, arrives=None):
                bank_free(t)
                for k in range(chunks):
                    if k % 8 == 0:
                        pe.wait_ge(lo_ready, (u + (k // 8 + 1)).value())
                    if arrives is not None:
                        pe.wait_ge(arrives, k + 1)
                    last = products(ps[:, t.slot(BANKS)], (u + k // 8).slot(SLOTS), slice(k % 8 * P, (k % 8 + 1) * P),
                                    hi[:, k], lo[:, k], k == 0, k == chunks - 1)
                    if k % 8 == 7:
                        last.then_inc(units_done, 1)

            def spread(n):
                pe.wait_ge(diag_ready, n)
                for b in range(BLK):
                    mm = pe.matmul(ps[:, B_BC, b * P:(b + 1) * P], ones[:], diag[:, b], start=True, stop=True)
                mm.then_inc(spread_done, 1)

            def token_sums(added, count):
                pe.wait_ge(added, count)
                for b in range(BLK):
                    mm = pe.matmul(ps[:, B_SUM, b:b + 1], acc[:, b * P:(b + 1) * P], ones[:, 0:1], start=True, stop=True)
                mm.then_inc(sums_done, 1)

            pe.wait_ge(par_in0, 16 * 9)
            pe.transpose(ps[:, B_PAR, 0:C_CAW], par_nat[0:C_CAW, 0], ident[0:C_CAW, 0:C_CAW]).then_inc(par_turned, 1)
            for c in range(DC):
                if c % HC == 0:
                    pe.wait_ge(x_in[c // HC], 16 * BLK)
                bank_free(At(c))
                for b in range(BLK):
                    mm = pe.transpose(ps[:, c % BANKS, b * P:(b + 1) * P], x_nat[:, b, c * P:(c + 1) * P], ident[:])
                mm.then_inc(x_turned, 1)
            pe.wait_ge(par_in1, 16 * 6)
            pe.wait_ge(par_ready, 1)
            n = CONV_W * HC // 2
            for j in range(2):
                pe.transpose(ps[:, B_PAR, C_CAW + j * n:C_CAW + (j + 1) * n], par_nat[0:n, 1 + j], ident[0:n, 0:n])
            n = 2 * FC
            for j in range(1 + FTAPS):
                mm = pe.transpose(ps[:, B_PAR2, j * n:(j + 1) * n], par_nat[0:n, 3 + j], ident[0:n, 0:n])
            mm.then_inc(par_turned, 1)
            spread(1)
            with pe.Fori(0, 2) as i:
                for j in range(4):
                    tile(At(U_B + 2 * j, i, 8), At(T_B + j, i, 4), xg_hi, xg_lo, arrives=xg_ready if j == 0 else None)
            for n in range(2):
                u = At(U_P + n)
                pe.wait_ge(lo_ready, (u + 1).value())
                for j in range(4):
                    g, mo = 2 * n + j // 2, j % 2
                    bank_free(At(T_P + 4 * n + j))
                    pe.wait_ge(pooled_ready, 2 * g + 2)
                    for k in range(2):
                        at = (2 * (j // 2) + k) * PGD + mo * P
                        last = products(ps[:, (T_P + j) % BANKS], u.slot(SLOTS), slice(at, at + P),
                                        pooled_hi[:, 2 * g + k], pooled_lo[:, 2 * g + k], k == 0, k == 1)
                last.then_inc(units_done, 1)
            with pe.Fori(0, HC // 2) as i:
                for j in range(4):
                    tile(At(U_A + 2 * j, i, 8), At(T_A + j, i, 4), xg_hi, xg_lo)

            def branch(first_u, first_t, n, hi, lo, ready, count):
                with pe.Fori(0, n // 4) as i:
                    for j in range(4):
                        tile(At(first_u + 3 * j, i, 12), At(first_t + 2 * j, i, 8), xg_hi, xg_lo)
                        if j == 0:
                            pe.wait_ge(ready, count)
                        tile(At(first_u + 3 * j + 2, i, 12), At(first_t + 2 * j + 1, i, 8), hi, lo, chunks=HC)

            branch(U_M1, T_M1, DC // 2, mixed_hi, mixed_lo, tiles_taken, T_P + HC)
            pe.wait_ge(mean_sum_ready, 1)
            pe.matmul(ps[:, B_BC], ones[:], acc[:], start=True, stop=True).then_inc(spread_done, 1)
            branch(U_M1 + 3 * DC // 2, T_M1 + DC, DC // 2, mixed_hi, mixed_lo, tiles_taken, T_P + HC)
            token_sums(squares_added, S_LN + HC)
            spread(2)
            branch(U_M2, T_M2, DC, a_hi, a_lo, a_ready, HC)
            with pe.Fori(0, DC // 4) as i:
                for j in range(4):
                    tile(At(U_O + 2 * j, i, 8), At(T_O + j, i, 4), xg_hi, xg_lo, arrives=merged_split if j == 0 else None)
            token_sums(tiles_taken, T_O + DC)
            spread(3)

            def up(u, t, c, arrives=None):
                for j in range(2):
                    tile(u + (4 * c + 2 * j), t + (2 * c + j), xg_hi, xg_lo, arrives=arrives if j == 0 else None)
                    if arrives is not None and j == 0:
                        token_sums(squares_added, S_X2 + DC)
                        spread(4)

            def down(u, t, half):
                for v in range(DC // 2):
                    pe.wait_ge(lo_ready, (u + (v + 1)).value())
                    for j in range(2):
                        bank_free(t + (2 * v + j))
                        for k in range(GRP):
                            at = k * 2 * P + j * P
                            last = products(ps[:, (t + (2 * v + j)).slot(BANKS)], (u + v).slot(SLOTS), slice(at, at + P),
                                            g_hi[:, half, k], g_lo[:, half, k], k == 0, k == GRP - 1)
                    last.then_inc(units_done, 1)

            for c in range(GRP):
                up(At(F_UP(0)), At(FT_UP(0)), c, arrives=x2g_ready if c == 0 else None)
            with pe.Fori(0, (NGRP - 1) // 2) as i:
                for s in range(2):
                    for c in range(GRP):
                        up(At(F_UP(1 + s), i, 48), At(FT_UP(1 + s), i, 48), c)
                    pe.wait_ge(g_ready, At(GRP * (1 + s), i, 2 * GRP).value())
                    down(At(F_DOWN(s), i, 48), At(FT_DOWN(s), i, 48), s)
            pe.wait_ge(g_ready, FC)
            pe.wait_ge(p_in, 16)
            for k in range(PLEC):
                for b in range(BLK):
                    mm = pe.transpose(ps[:, B_PAR + k, b * P:(b + 1) * P], p_nat[:, b, k * P:(k + 1) * P], ident[:])
            mm.then_inc(p_turned, 1)
            down(At(F_DOWN(NGRP - 1)), At(FT_DOWN(NGRP - 1)), 0)
            pe.wait_ge(p_ready, PLEC)
            for n in range(4):
                pe.wait_ge(lo_ready, U_L + n + 1)
                for j in range(4):
                    if n == 0:
                        pe.wait_ge(tiles_taken, T_G - BANKS + 1 + j)
                    else:
                        pe.wait_ge(ple_taken, 4 * n + j - 3)
                    for k in range(PLEC):
                        at = k * TOK + j * P
                        last = products(ps[:, j], (U_L + n) % SLOTS, slice(at, at + P), p_hi[:, k], p_lo[:, k], k == 0, k == PLEC - 1)
                last.then_inc(units_done, 1)
                if n == 0:
                    token_sums(squares_added, S_F + DC)
                    spread(5)
            pe.wait_ge(ple_taken, DC)
            with pe.Fori(0, DC // 4) as i:
                for j in range(4):
                    tile(At(U_G + 2 * j, i, 8), At(T_G + j, i, 4), x3_hi, x3_lo, arrives=x3_split if j == 0 else None)
            token_sums(squares_added, S_E + DC)
            spread(6)
            pe.wait_ge(tiles_taken, T_G + DC)
            for q in range(DC // 4):
                pe.wait_ge(y_ready, 4 * q + 4)
                for b in range(BLK):
                    if q > 0:
                        pe.wait_ge(y_taken, BLK * (q - 1) + b + 1)
                    for j in range(4):
                        mm = pe.transpose(ps[:, b, j * P:(j + 1) * P], x2_back[:, 4 * q + j, b * P:(b + 1) * P], ident[:])
                    mm.then_inc(y_turned, 1)

        @block.scalar
        def _(act):
            f = act.activation

            def split(u):
                act.wait_ge(raw_in[u.slot(RAW)], u.raw_count().value())
                f(w_hi[:, u.slot(SLOTS)], w_raw[:, u.slot(RAW)], ACT.Copy).then_inc(hi_ready, 1)

            def step(u, ahead=True):
                act.wait_ge(units_done, (u + 1).value())
                if ahead:
                    split(u + SLOTS)

            def standard_deviation(n, total, src):
                f(std[:], src, ACT.Sqrt, bias=eps[:], scale=1.0 / total).then_inc(std_ready, 1)

            for j, (v, n) in enumerate(((mix_pre_g, DC), (mix_post_g, DC), (ffn_pre_g, DC), (ffn_post_g, DC), (ple_post_g, DC),
                                        (conv_a_b, HC), (ln_a_g, HC), (ln_a_b, HC), (pool_scale, HC))):
                row = j * DC if j < 5 else C_CAB + (j - 5) * HC
                act.dma_start(par_nat[row:row + n, 0], v.rearrange("(c p) -> c p", p=P)).then_inc(par_in0, 16)
            taps = conv_a_w.rearrange("k (c p) -> (k c) p", p=P)
            n = CONV_W * HC // 2
            for j in range(2):
                act.dma_start(par_nat[0:n, 1 + j], taps[j * n:(j + 1) * n]).then_inc(par_in1, 16)
            act.dma_start(par_nat[0:2 * FC, 3], conv_f_b.rearrange("(c p) -> c p", p=P)).then_inc(par_in1, 16)
            for k in range(FTAPS):
                act.dma_start(par_nat[0:2 * FC, 4 + k], conv_f_w[k].rearrange("(c p) -> c p", p=P)).then_inc(par_in1, 16)

            act.wait_ge(par_ready, 1)
            for h in range(2):
                act.wait_ge(x_in[h], 16 * BLK)
                for b in range(BLK):
                    if h + b > 0:
                        act.wait_ge(x_squares, h * BLK + b)
                    f(sq[:].rearrange("p a t -> p (a t)"), x_nat[:, b, h * H:(h + 1) * H], ACT.Square,
                      accum_out=x_sums[:, h * BLK + b:h * BLK + b + 1]).then_inc(x_squares, 1)
                    for c in (2 * (h * BLK + b), 2 * (h * BLK + b) + 1):
                        act.wait_ge(x_turned, c + 1)
                        f(xg_hi[:, c], ps[:, c % BANKS], ACT.Identity, scale=par[:, C_MIXPRE + c:C_MIXPRE + c + 1]).then_inc(xg_hi_ready, 1)
                    if h == 1:
                        split(At(b))
            act.wait_ge(x_sums_ready, 1)
            act.wait_ge(consts_ready, 3)
            standard_deviation(1, D, x_sum[:])

            for c in range(HC):
                step(At(U_B + 2 * c))
                step(At(U_B + 2 * c + 1))
                act.wait_ge(pool_f_ready, c + 1)
                f(pooled_hi[:, c], pool_f[:], ACT.Copy).then_inc(pooled_hi_ready, 1)
            for n in range(2):
                step(At(U_P + n))
                for j in range(4):
                    c = 4 * n + j
                    f(mixed_hi[:, c], ps[:, (T_P + c) % BANKS], ACT.Identity, scale=par[:, C_PSC + c:C_PSC + c + 1]).then_inc(mixed_hi_ready, 1)

            def sigmoid(t):
                act.wait_ge(tiles_taken, (t + 1).value())
                f(sig[:], scaled[:], ACT.Sigmoid).then_inc(sigmoid_ready, 1)

            with act.Fori(0, HC // 2) as i:
                for j in range(2):
                    u = At(U_A + 4 * j, i, 8)
                    step(u)
                    step(u + 1)
                    sigmoid(At(T_A + 2 * j, i, 4))
                    step(u + 2)
                    step(u + 3)
            with act.Fori(0, DC // 8) as i:
                for j in range(4):
                    u = At(U_M1 + 3 * j, i, 12)
                    step(u)
                    step(u + 1)
                    sigmoid(At(T_M1 + 2 * j, i, 8))
                    step(u + 2)
            with act.Fori(0, DC // 8) as i:
                for j in range(4):
                    u = At(U_M1 + 3 * DC // 2 + 3 * j, i, 12)
                    step(u)
                    act.wait_ge(centred, At(j + 1, i, 4).value())
                    f(sq[:, j % 2], a_conv[:, bass.ds(i * 4 + j, 1), PAD:PAD + TOK], ACT.Square).then_inc(squares_ready, 1)
                    step(u + 1)
                    sigmoid(At(T_M1 + DC + 2 * j, i, 8))
                    step(u + 2)
            act.wait_ge(sums_done, 1)
            standard_deviation(2, H, ps[:, B_SUM, 0:BLK])
            for c in range(HC):
                act.wait_ge(ln_scaled, c + 1)
                if c > 0:
                    act.wait_ge(a_ready, c)
                f(tmp[:], scaled[:] if c % 2 == 0 else conv_acc[:], ACT.Silu, bias=par[:, C_LNB + c:C_LNB + c + 1]).then_inc(silu_ready, 1)
                act.wait_ge(silu_ready, c + 1)
                f(a_hi[:, c], tmp[:], ACT.Copy).then_inc(a_hi_ready, 1)
            with act.Fori(0, DC // 4) as i:
                for j in range(4):
                    u = At(U_M2 + 3 * j, i, 12)
                    step(u)
                    step(u + 1)
                    sigmoid(At(T_M2 + 2 * j, i, 8))
                    step(u + 2)
            for c in range(DC):
                act.wait_ge(merged_ready, c + 1)
                f(xg_hi[:, c], merged[:, c], ACT.Copy).then_inc(merged_hi_ready, 1)

            with act.Fori(0, DC // 4) as i:
                for j in range(4):
                    u = At(U_O + 2 * j, i, 8)
                    step(u)
                    step(u + 1)
                    act.wait_ge(tiles_taken, At(T_O + j - 1, i, 4).value())
                    f(og[:, bass.ds(i * 4 + j, 1)], ps[:, j:j + 1], ACT.Identity, scale=par[:, bass.ds(i * 4 + (C_MIXPOST + j), 1)])
                    f(sq[:, j % 2], ps[:, j], ACT.Square).then_inc(squares_ready, 1)
            act.wait_ge(sums_done, 2)
            standard_deviation(3, D, ps[:, B_SUM, 0:BLK])
            for c in range(DC):
                act.wait_ge(x2_ready, c + 1)
                f(xg_hi[:, c], x2[:, c], ACT.Identity, scale=par[:, C_FFNPRE + c:C_FFNPRE + c + 1]).then_inc(x2g_hi_ready, 1)
                if c >= 2:
                    act.wait_ge(squares_added, S_X2 + c - 1)
                f(sq[:, c % 2], x2[:, c], ACT.Square).then_inc(squares_ready, 1)

            def param(base, q):
                return par[:, q.c + base:q.c + base + 1] if q.i is None else par[:, bass.ds(q.i * q.k + (q.c + base), 1)]

            def up(u, t, q, half, first=False):
                def high(c):
                    act.wait_ge(ff_ready, (q + (c + 1)).value())
                    f(g_hi[:, half, c], ff_prod[:], ACT.Copy).then_inc(g_hi_ready, 1)

                def first_tap(dst, src, c, j):
                    act.wait_ge(tiles_taken, (t + (2 * c + j + 1)).value())
                    f(dst[:], src[:, 0:TOK], ACT.Identity, scale=param(C_CFW + j * FC, q + c),
                      bias=param(C_CFB + j * FC, q + c)).then_inc(first_tap_ready, 1)

                for c in range(GRP):
                    step(u + 4 * c)
                    if c > 0:
                        high(c - 1)
                    step(u + (4 * c + 1))
                    if first and c == 0:
                        act.wait_ge(sums_done, 3)
                        standard_deviation(4, D, ps[:, B_SUM, 0:BLK])
                    first_tap(gate_c, up_gate, c, 0)
                    step(u + (4 * c + 2))
                    act.wait_ge(gate_conv_ready, (q + (c + 1)).value())
                    f(gelu_g[:], gate_c[:], ACT.Gelu_apprx_tanh).then_inc(gelu_ready, 1)
                    step(u + (4 * c + 3))
                    first_tap(val_c, up_val, c, 1)
                high(GRP - 1)

            up(At(F_UP(0)), At(FT_UP(0)), At(0), 0, first=True)
            with act.Fori(0, (NGRP - 1) // 2) as i:
                for s in range(2):
                    up(At(F_UP(1 + s), i, 48), At(FT_UP(1 + s), i, 48), At(GRP * (1 + s), i, 2 * GRP), 1 - s)
                    for v in range(DC // 2):
                        step(At(F_DOWN(s) + v, i, 48))
            act.wait_ge(p_turned, 1)
            for k in range(PLEC):
                f(p_hi[:, k], ps[:, B_PAR + k], ACT.Copy).then_inc(p_hi_ready, 1)
            for v in range(DC // 2):
                step(At(F_DOWN(NGRP - 1) + v))
                for j in range(2):
                    m = 2 * v + j
                    act.wait_ge(tiles_taken, FT_DOWN(NGRP - 1) + m + 1)
                    if m >= 2:
                        act.wait_ge(squares_added, S_F + m - 1)
                    f(sq[:, m % 2], f_acc[:, m], ACT.Square).then_inc(squares_ready, 1)
            for n in range(4):
                step(At(U_L + n))
                for j in range(4):
                    f(e_buf[:, 4 * n + j], ps[:, j], ACT.Copy).then_inc(ple_taken, 1)
                if n == 0:
                    act.wait_ge(sums_done, 4)
                    standard_deviation(5, D, ps[:, B_SUM, 0:BLK])
                for c in range(4 * n, 4 * n + 4):
                    act.wait_ge(x3_ready, c + 1)
                    f(x3_hi[:, c], x2_back[:, c], ACT.Copy).then_inc(x3_hi_ready, 1)

            def gate(u, t, m, j, ahead=True):
                step(u, ahead)
                step(u + 1, ahead)
                f(sig[:], ps[:, j], ACT.Sigmoid).then_inc(sigmoid_ready, 1)
                act.wait_ge(tiles_taken, (t + 1).value())
                act.wait_ge(squares_added, (m + (S_E + j - 1)).value())
                src = e_buf[:, bass.ds(m.i * m.k + (m.c + j), 1)] if m.i is not None else e_buf[:, m.c + j:m.c + j + 1]
                f(sq[:, j % 2], src, ACT.Square).then_inc(squares_ready, 1)

            with act.Fori(0, DC // 4 - 1) as i:
                for j in range(4):
                    gate(At(U_G + 2 * j, i, 8), At(T_G + j, i, 4), At(0, i, 4), j)
            for j in range(4):
                gate(At(U_END - 8 + 2 * j), At(T_G + DC - 4 + j), At(DC - 4), j, ahead=j < 2)
            act.wait_ge(sums_done, 5)
            standard_deviation(6, D, ps[:, B_SUM, 0:BLK])
            for q in range(DC // 4):
                if q >= 2:
                    act.wait_ge(out_done[q % 2], 16)
                for b in range(BLK):
                    act.wait_ge(y_turned, BLK * q + b + 1)
                    f(y_nat[:, q % 2, b], ps[:, b], ACT.Copy).then_inc(y_taken, 1)

        @block.vector
        def _(dve):
            op = Tally(dve, dve_chain)
            as_f32 = lambda ap: ap.bitcast(F32)
            flat = lambda ap: ap.rearrange("p a t -> p (a t)")

            def split(u):
                dve.wait_ge(hi_ready, (u + 1).value())
                s = u.slot(SLOTS)
                dve.tensor_tensor(w_lo[:, s], w_raw[:, u.slot(RAW)], as_f32(w_hi[:, s]), ALU.subtract).then_inc(lo_ready, 1)

            def step(u):
                split(u + SLOTS)

            def scale_tile(dst, t):
                dve.tensor_tensor(dst, ps[:, t.slot(BANKS)], r_bc[:], ALU.mult).then_inc(tiles_taken, 1)

            def factor(n, dst=r_bc):
                dve.wait_ge(std_ready, n)
                op(dve.reciprocal(rstd[:], std[:]))
                op.settle()
                for b in range(BLK):
                    ins = dve.tensor_scalar(diag[:, b], ident[:], rstd[:, b:b + 1], None, ALU.mult)
                ins.then_inc(diag_ready, 1)
                dve.wait_ge(spread_done, n if n == 1 else n + 1)
                op(dve.tensor_copy(dst[:], ps[:, B_BC]))
                op.settle()

            def clear_acc():
                op(dve.memset(acc[:], 0.0))
                op.settle()

            def low(dst, src, hi, done):
                dve.tensor_tensor(dst, src, as_f32(hi), ALU.subtract).then_inc(done, 1)

            def scaled_low(dst, src, scale, hi, done):
                dve.scalar_tensor_tensor(out=dst, in0=src, scalar=scale, in1=as_f32(hi), op0=ALU.mult, op1=ALU.subtract).then_inc(done, 1)

            def normed(dst, src, g):
                op(dve.scalar_tensor_tensor(out=dst, in0=src, scalar=g, in1=r_bc[:], op0=ALU.mult, op1=ALU.mult))

            def add_squares(slot, made, added):
                dve.wait_ge(squares_ready, made)
                dve.wait_ge(squares_added, added)
                dve.tensor_tensor(acc[:], acc[:], sq[:, slot], ALU.add).then_inc(squares_added, 1)

            dve.wait_ge(par_turned, 1)
            dve.tensor_copy(par[:, 0:C_CAW], ps[:, B_PAR, 0:C_CAW]).then_inc(par_ready, 1)
            dve.wait_ge(par_ready, 1)
            for c in range(DC):
                dve.wait_ge(xg_hi_ready, c + 1)
                scaled_low(xg_lo[:, c], ps[:, c % BANKS], par[:, C_MIXPRE + c:C_MIXPRE + c + 1], xg_hi[:, c], xg_ready)
                dve.tensor_copy(xt[:, c], ps[:, c % BANKS]).then_inc(tiles_taken, 1)
                if c >= HC and c % 2 == 1:
                    split(At((c - HC) // 2))
            dve.wait_ge(x_squares, 2 * BLK)
            dve.tensor_tensor(x_sum[:], x_sums[:, 0:BLK], x_sums[:, BLK:2 * BLK], ALU.add).then_inc(x_sums_ready, 1)
            dve.wait_ge(par_turned, 2)
            op(dve.tensor_copy(par[:, C_CAW:C_CFB], ps[:, B_PAR, C_CAW:C_CFB]))
            op(dve.tensor_copy(par[:, C_CFB:C_ALL], ps[:, B_PAR2, 0:C_ALL - C_CFB]))
            dve.wait_ge(consts_ready, 3 + PPAD)
            factor(1)

            op(dve.memset(u_pool[:, 0:PPAD], 0.0))
            dve.wait_ge(xt_out, 16)

            def pooled_low(c):
                dve.wait_ge(pooled_hi_ready, c + 1)
                low(pooled_lo[:, c], pool_f[:], pooled_hi[:, c], pooled_ready)

            for c in range(HC):
                w = WINDOWS[c // 2]
                step(At(U_B + 2 * c))
                if c > 0:
                    pooled_low(c - 1)
                step(At(U_B + 2 * c + 1))
                scale_tile(u_pool[:, PPAD:], At(T_B + c))
                dve.wait_ge(tiles_taken, T_B + c + 1)
                have, s = 1, u_pool
                while have < w:
                    dst = s_pool[:, have.bit_length() % 2]
                    op.settle()
                    op(dve.tensor_tensor(dst[:, 2 * have - 1:], s[:, 2 * have - 1:], s[:, have - 1:PPAD + TOK - have], ALU.add))
                    s, have = dst, 2 * have
                op.settle()
                op(dve.tensor_tensor(pool_f[:, 0:w - 1], s[:, PPAD:PPAD + w - 1], inv_count[:, 0:w - 1], ALU.mult))
                op.settle()
                op(dve.tensor_tensor(pool_f[:, 0:w - 1], pool_f[:, 0:w - 1], u_pool[:, PPAD:PPAD + w - 1], ALU.subtract))
                dve.scalar_tensor_tensor(out=pool_f[:, w - 1:], in0=s[:, PPAD + w - 1:], scalar=1.0 / w,
                                         in1=u_pool[:, PPAD + w - 1:], op0=ALU.mult, op1=ALU.subtract).then_inc(pool_f_ready, 1)
                dve.wait_ge(pool_f_ready, c + 1)
            pooled_low(HC - 1)
            for n in range(2):
                step(At(U_P + n))
                for j in range(4):
                    c = 4 * n + j
                    dve.wait_ge(mixed_hi_ready, c + 1)
                    scaled_low(mixed_lo[:, c], ps[:, (T_P + c) % BANKS], par[:, C_PSC + c:C_PSC + c + 1], mixed_hi[:, c], tiles_taken)

            op(dve.memset(a_conv[:, :, 0:PAD], 0.0))
            clear_acc()

            def conv_taps(c, first, last):
                chunk = lambda k: flat(a_conv[:, bass.ds(c, 1), k:k + TOK])
                for k in range(first, last):
                    weight = par[:, bass.ds(c + (C_CAW + k * HC), 1)]
                    op.settle()
                    if k == 0:
                        op(dve.tensor_scalar(conv_acc[:], chunk(0), weight, par[:, bass.ds(c + C_CAB, 1)], ALU.mult, ALU.add))
                    else:
                        dst = chunk(PAD) if k == CONV_W - 1 else conv_acc[:]
                        op(dve.scalar_tensor_tensor(out=dst, in0=chunk(k), scalar=weight, in1=conv_acc[:], op0=ALU.mult, op1=ALU.add))
                if last == CONV_W:
                    op.settle()
                    op(dve.tensor_tensor(acc[:], acc[:], chunk(PAD), ALU.add))

            per = 2 + CONV_W + 1
            with dve.Fori(0, HC // 2) as i:
                op.enter(i, per)
                for j in range(2):
                    u, t = At(U_A + 4 * j, i, 8), At(T_A + 2 * j, i, 4)
                    taps = ((0, 0), (0, 8), (8, 16), (16, 24), (24, CONV_W))[1:] if j == 1 else 4 * ((0, 0),)
                    step(u)
                    conv_taps(i, *taps[0])
                    step(u + 1)
                    scale_tile(scaled[:], t)
                    conv_taps(i, *taps[1])
                    step(u + 2)
                    conv_taps(i, *taps[2])
                    step(u + 3)
                    scale_tile(tmp[:], t + 1)
                    dve.wait_ge(tiles_taken, (t + 2).value())
                    dve.wait_ge(sigmoid_ready, At(G_A + j + 1, i, 2).value())
                    op(dve.tensor_tensor(flat(a_conv[:, bass.ds(i * 2 + j, 1), PAD:]), tmp[:], sig[:], ALU.mult))
                    conv_taps(i, *taps[3])
            op.leave(HC // 2, per)

            def gated(dst, t, sigmoids, done):
                dve.wait_ge(sigmoid_ready, sigmoids.value())
                dve.tensor_tensor(dst, ps[:, t.slot(BANKS)], sig[:], ALU.mult).then_inc(done, 1)

            per = 2 * (CONV_W + 1)
            with dve.Fori(0, DC // 8) as i:
                op.enter(i, per)
                for j in range(4):
                    c = i * 2 + (HC // 2 + j // 2)
                    taps = ((0, 5), (5, 10), (10, 15)) if j % 2 == 0 else ((15, 21), (21, 26), (26, CONV_W))
                    u, t = At(U_M1 + 3 * j, i, 12), At(T_M1 + 2 * j, i, 8)
                    step(u)
                    conv_taps(c, *taps[0])
                    step(u + 1)
                    scale_tile(scaled[:], t)
                    conv_taps(c, *taps[1])
                    step(u + 2)
                    gated(flat(merged[:, bass.ds(i * 4 + j, 1)]), t + 1, At(G_M1 + j + 1, i, 4), tiles_taken)
                    conv_taps(c, *taps[2])
            op.leave(DC // 8, per)
            op.settle()
            dve.tensor_scalar(acc[:], acc[:], 1.0 / H, None, ALU.mult).then_inc(mean_sum_ready, 1)
            dve.wait_ge(spread_done, 2)
            op(dve.tensor_copy(tmp[:], ps[:, B_BC]))
            clear_acc()
            with dve.Fori(0, DC // 8) as i:
                for j in range(4):
                    u, t = At(U_M1 + 3 * DC // 2 + 3 * j, i, 12), At(T_M1 + DC + 2 * j, i, 8)
                    step(u)
                    chunk = flat(a_conv[:, bass.ds(i * 4 + j, 1), PAD:])
                    dve.tensor_tensor(chunk, chunk, tmp[:], ALU.subtract).then_inc(centred, 1)
                    step(u + 1)
                    scale_tile(scaled[:], t)
                    dve.wait_ge(squares_ready, At(Q_LN + j + 1, i, 4).value())
                    dve.tensor_tensor(acc[:], acc[:], sq[:, j % 2], ALU.add).then_inc(squares_added, 1)
                    step(u + 2)
                    gated(flat(merged[:, bass.ds(i * 4 + (DC // 2 + j), 1)]), t + 1, At(G_M1 + DC // 2 + j + 1, i, 4), tiles_taken)
                    dve.wait_ge(squares_added, At(S_LN + j + 1, i, 4).value())
            factor(2, dst=acc)
            n_buf = (scaled, conv_acc)
            for c in range(HC):
                if c >= 2:
                    dve.wait_ge(silu_ready, c - 1)
                dve.scalar_tensor_tensor(out=n_buf[c % 2][:], in0=a_conv[:, c, PAD:], scalar=par[:, C_LNG + c:C_LNG + c + 1],
                                         in1=acc[:], op0=ALU.mult, op1=ALU.mult).then_inc(ln_scaled, 1)
                if c > 0:
                    dve.wait_ge(a_hi_ready, c)
                    low(a_lo[:, c - 1], tmp[:], a_hi[:, c - 1], a_ready)
            dve.wait_ge(a_hi_ready, HC)
            low(a_lo[:, HC - 1], tmp[:], a_hi[:, HC - 1], a_ready)

            with dve.Fori(0, DC // 4) as i:
                for j in range(4):
                    u, t = At(U_M2 + 3 * j, i, 12), At(T_M2 + 2 * j, i, 8)
                    step(u)
                    step(u + 1)
                    scale_tile(scaled[:], t)
                    step(u + 2)
                    gated(tmp[:], t + 1, At(G_M2 + j + 1, i, 4), tiles_taken)
                    dve.wait_ge(tiles_taken, (t + 2).value())
                    m = flat(merged[:, bass.ds(i * 4 + j, 1)])
                    dve.tensor_tensor(m, m, tmp[:], ALU.add).then_inc(merged_ready, 1)
            clear_acc()
            for c in range(DC):
                dve.wait_ge(merged_hi_ready, c + 1)
                low(xg_lo[:, c], merged[:, c], xg_hi[:, c], merged_split)

            with dve.Fori(0, DC // 4) as i:
                for j in range(4):
                    u, t = At(U_O + 2 * j, i, 8), At(T_O + j, i, 4)
                    step(u)
                    step(u + 1)
                    dve.wait_ge(squares_ready, At(Q_O + j + 1, i, 4).value())
                    dve.wait_ge(tiles_taken, t.value())
                    dve.tensor_tensor(acc[:], acc[:], sq[:, j % 2], ALU.add).then_inc(tiles_taken, 1)
            factor(3)
            clear_acc()
            dve.wait_ge(xt_in, 16)

            t_buf = (scaled, conv_acc)

            def x2_tail(c):
                dve.wait_ge(x2g_hi_ready, c + 1)
                scaled_low(xg_lo[:, c], x2[:, c], par[:, C_FFNPRE + c:C_FFNPRE + c + 1], xg_hi[:, c], x2g_ready)
                add_squares(c % 2, Q_X2 + c + 1, S_X2 + c)

            for c in range(DC):
                op(dve.tensor_tensor(t_buf[c % 2][:], og[:, c], r_bc[:], ALU.mult))
                op.settle()
                dve.tensor_tensor(x2[:, c], xt[:, c], t_buf[c % 2][:], ALU.add).then_inc(x2_ready, 1)
                if c > 0:
                    x2_tail(c - 1)
            x2_tail(DC - 1)

            op(dve.memset(up_gate[:, 0:2], 0.0))
            op(dve.memset(up_val[:, 0:2], 0.0))

            def param(base, q):
                return par[:, q.c + base:q.c + base + 1] if q.i is None else par[:, bass.ds(q.i * q.k + (q.c + base), 1)]

            def up(u, t, q, half, first=False):
                def last_taps(dst, src, c, j, tally):
                    dve.wait_ge(first_tap_ready, At(2 * (q.c + c) + j + 1, q.i, 2 * q.k).value())
                    dve.wait_ge(tiles_taken, (t + (2 * c + j + 1)).value())
                    op(dve.scalar_tensor_tensor(out=dst[:], in0=src[:, 1:1 + TOK], scalar=param(C_CFW + 2 * FC + j * FC, q + c),
                                                in1=dst[:], op0=ALU.mult, op1=ALU.add))
                    op.settle()
                    tally(dve.scalar_tensor_tensor(out=dst[:], in0=src[:, 2:2 + TOK], scalar=param(C_CFW + 4 * FC + j * FC, q + c),
                                                   in1=dst[:], op0=ALU.mult, op1=ALU.add))

                def product(c):
                    last_taps(val_c, up_val, c, 1, op)
                    op.settle()
                    dve.wait_ge(gelu_ready, (q + (c + 1)).value())
                    dve.tensor_tensor(ff_prod[:], gelu_g[:], val_c[:], ALU.mult).then_inc(ff_ready, 1)

                def product_low(c):
                    dve.wait_ge(g_hi_ready, (q + (c + 1)).value())
                    low(g_lo[:, half, c], ff_prod[:], g_hi[:, half, c], g_ready)

                for c in range(GRP):
                    step(u + 4 * c)
                    if c > 0:
                        product(c - 1)
                    step(u + (4 * c + 1))
                    if c > 0:
                        product_low(c - 1)
                    if first and c == 0:
                        factor(4)
                    scale_tile(up_gate[:, 2:], t + 2 * c)
                    step(u + (4 * c + 2))
                    last_taps(gate_c, up_gate, c, 0, lambda ins: ins.then_inc(gate_conv_ready, 1))
                    step(u + (4 * c + 3))
                    scale_tile(up_val[:, 2:], t + (2 * c + 1))
                product(GRP - 1)
                product_low(GRP - 1)

            def down(u, t, last=False):
                for v in range(DC // 2):
                    step(u + v)
                    for j in range(2):
                        m = 2 * v + j
                        dve.tensor_tensor(f_acc[:, m], f_acc[:, m], ps[:, (t + m).slot(BANKS)], ALU.add).then_inc(tiles_taken, 1)
                        if last and m > 0:
                            add_squares((m - 1) % 2, Q_F + m, S_F + m - 1)
                if last:
                    add_squares((DC - 1) % 2, Q_F + DC, S_F + DC - 1)

            up(At(F_UP(0)), At(FT_UP(0)), At(0), 0, first=True)
            dve.wait_ge(f_zero, 1)
            per = 2 * GRP * 3
            with dve.Fori(0, (NGRP - 1) // 2) as i:
                op.enter(i, per)
                for s in range(2):
                    up(At(F_UP(1 + s), i, 48), At(FT_UP(1 + s), i, 48), At(GRP * (1 + s), i, 2 * GRP), 1 - s)
                    down(At(F_DOWN(s), i, 48), At(FT_DOWN(s), i, 48))
            op.leave((NGRP - 1) // 2, per)
            for k in range(PLEC):
                dve.wait_ge(p_hi_ready, k + 1)
                low(p_lo[:, k], ps[:, B_PAR + k], p_hi[:, k], p_ready)
            clear_acc()
            down(At(F_DOWN(NGRP - 1)), At(FT_DOWN(NGRP - 1)), last=True)

            def x3_low(c):
                dve.wait_ge(x3_hi_ready, c + 1)
                low(x3_lo[:, c], x2_back[:, c], x3_hi[:, c], x3_split)

            for n in range(4):
                step(At(U_L + n))
                if n == 0:
                    factor(5)
                    clear_acc()
                    dve.wait_ge(x2_in, 16)
                for c in range(4 * n, 4 * n + 4):
                    normed(t_buf[c % 2][:], f_acc[:, c], par[:, C_FFNPOST + c:C_FFNPOST + c + 1])
                    op.settle()
                    dve.tensor_tensor(x2_back[:, c], x2_back[:, c], t_buf[c % 2][:], ALU.add).then_inc(x3_ready, 1)
                    if c > 0:
                        x3_low(c - 1)
            x3_low(DC - 1)

            def gate(u, t, m, j, ahead=True):
                if ahead:
                    step(u)
                    step(u + 1)
                n = m + j
                e = flat(e_buf[:, bass.ds(m.i * m.k + n.c, 1)]) if m.i is not None else e_buf[:, n.c]
                dve.wait_ge(sigmoid_ready, (n + (G_G + 1)).value())
                dve.tensor_tensor(e, e, sig[:], ALU.mult).then_inc(tiles_taken, 1)
                add_squares(j % 2, (n + (Q_E + 1)).value(), (n + S_E).value())

            with dve.Fori(0, DC // 4 - 1) as i:
                for j in range(4):
                    gate(At(U_G + 2 * j, i, 8), At(T_G + j, i, 4), At(0, i, 4), j)
            for j in range(4):
                gate(At(U_END - 8 + 2 * j), At(T_G + DC - 4 + j), At(DC - 4), j, ahead=j < 2)
            factor(6)
            for c in range(DC):
                normed(t_buf[c % 2][:], e_buf[:, c], par[:, C_PLEPOST + c:C_PLEPOST + c + 1])
                op.settle()
                dve.tensor_tensor(x2_back[:, c], x2_back[:, c], t_buf[c % 2][:], ALU.add).then_inc(y_ready, 1)


NAMES = ["x", "p", "mix_pre_g", "w_in", "conv_a_w", "conv_a_b", "ln_a_g", "ln_a_b", "w_a_out", "pool_w", "pool_scale",
         "w_b_out", "w_o", "mix_post_g", "ffn_pre_g", "w_up", "conv_f_w", "conv_f_b", "w_down", "ffn_post_g", "w_ple",
         "w_ple_gate", "ple_post_g"]


def kernel(**inputs):
    import concourse.bacc as bacc
    from concourse.bass_utils import run_bass_kernel_spmd

    nc = bacc.Bacc("TRN2", target_bir_lowering=False, num_devices=1)
    arrays, args = {}, []
    for name in NAMES:
        a = np.ascontiguousarray(inputs[name])
        arrays[f"in_{name}"] = a
        args.append(nc.dram_tensor(f"in_{name}", a.shape, mybir.dt.from_np(a.dtype), kind="ExternalInput").ap())
    out = nc.dram_tensor("out_0", (1, TOK, D), F32, kind="ExternalOutput").ap()
    build(nc, *args, out)
    r = run_bass_kernel_spmd(nc, [arrays], core_ids=[0])
    return r.results[0]["out_0"]
```

```python
from contextlib import ExitStack

import numpy as np

import concourse.bass as bass
from concourse import mybir

F32 = mybir.dt.float32
F32R = mybir.dt.float32r
ALU = mybir.AluOpType
ACT = mybir.ActivationFunctionType
AX = mybir.AxisListType

P = 128
TOK = 512
BLK = TOK // P
D = 2048
DC = D // P
W = 512
NG = D // W
H = D // 2
HC = H // P
FF = 5632
FC = FF // P
CONV_W = 31
PAD = CONV_W - 1
WINDOWS = (2, 4, 8, 16)
PGD = H // len(WINDOWS)
PPAD = 16
FTAPS = 3
PLE = 256
PLEC = PLE // P
EPS = 1e-6
GRP = 4
NGRP = FC // GRP

UNIT = 8 * P
RAW, SLOTS = 2, 4

U_A = 0
U_B = U_A + 4 * HC
U_M1 = U_B + 2 * HC + 2
U_M2 = U_M1 + 3 * DC
U_O = U_M2 + 3 * DC
U_F = U_O + 2 * DC
U_L = U_F + 4 * FC + 8 * NGRP
U_G = U_L + 4
U_END = U_G + 2 * DC
T_A = 0
T_B = T_A + 2 * HC
T_M1 = T_B + HC + 4
T_M2 = T_M1 + 2 * DC
T_O = T_M2 + 2 * DC
T_F = T_O + DC
T_G = T_F + 2 * FC + DC * NGRP
F_UP = lambda j: U_F if j == 0 else U_F + 4 * GRP + 24 * (j - 1)
F_DOWN = lambda j: U_F + 4 * GRP + 24 * j + (4 * GRP if j < NGRP - 1 else 0)
FT_UP = lambda j: T_F if j == 0 else T_F + 2 * GRP + 24 * (j - 1)
FT_DOWN = lambda j: T_F + 2 * GRP + 24 * j + (2 * GRP if j < NGRP - 1 else 0)
G_A, G_M1, G_M2, G_G = 0, HC, HC + DC, HC + 2 * DC
Q_LN, Q_O, Q_F, Q_E = 0, HC, HC + DC, HC + 2 * DC

C_MIXPRE, C_FFNPRE, C_CAB = 0, DC, 2 * DC
C_LNG = C_CAB + HC
C_LNB = C_LNG + HC
C_PSC = C_LNB + HC
C_CAW = C_PSC + HC
C_CFB = C_CAW + CONV_W * HC
C_CFW = C_CFB + 2 * FC
C_ALL = C_CFW + FTAPS * 2 * FC


class At:

    def __init__(self, c, i=None, k=0):
        self.c, self.i, self.k = c, i, k

    def __add__(self, n):
        return At(self.c + n, self.i, self.k)

    def value(self):
        return self.c if self.i is None or self.k == 0 else self.i * self.k + self.c

    def slot(self, n):
        assert self.k % n == 0
        return self.c % n

    def raw_count(self):
        assert self.k % RAW == 0
        return At(16 * (self.c // RAW + 1), self.i, 16 * self.k // RAW)


class Tally:

    def __init__(self, eng, sem):
        self.eng, self.sem, self.at = eng, sem, At(0)

    def __call__(self, ins):
        ins.then_inc(self.sem, 1)
        self.at = self.at + 1

    def settle(self, but=0):
        self.eng.wait_ge(self.sem, (self.at + -but).value())

    def enter(self, i, per, start=0):
        self.base = self.at.c - start * per
        self.at = At(self.base, i, per)

    def leave(self, n, per, start=0):
        assert self.at.c - self.base == per, f"the loop adds {self.at.c - self.base}, not {per}"
        self.at = At(self.base + n * per)


def build(nc, x, p, mix_pre_g, w_in, conv_a_w, conv_a_b, ln_a_g, ln_a_b, w_a_out, pool_w, pool_scale, w_b_out,
          w_o, mix_post_g, ffn_pre_g, w_up, conv_f_w, conv_f_b, w_down, ffn_post_g, w_ple, w_ple_gate,
          ple_post_g, out):
    x2_dram = nc.dram_tensor("x2_dram", (P, NG, BLK, W), F32, kind="Internal").ap()
    rows_of = lambda a: a.rearrange("a (b t) (n f) -> t n (a b) f", t=P, f=W)
    ctx = ExitStack()
    with ctx:
        sem = lambda name: ctx.enter_context(nc.semaphore(name))

        cursor = [16512]

        def region(nbytes):
            at = cursor[0]
            cursor[0] += (nbytes + 63) // 64 * 64
            return at

        def place(name, shape, dt, offset):
            return nc.alloc_sbuf_tensor_at(name, shape, dt, offset=offset)

        FULL = DC * TOK * 4
        r_raw, r_whi, r_wlo = region(RAW * UNIT * 4), region(SLOTS * UNIT * 4), region(SLOTS * UNIT * 4)
        r1, r2, r3, r4 = region(FULL), region(FULL), region(FULL), region(FULL)
        r5 = region(HC * (PAD + TOK) * 4)
        w_raw = place("w_raw", [P, RAW, UNIT], F32, r_raw)
        w_hi = place("w_hi", [P, SLOTS, UNIT], F32R, r_whi)
        w_lo = place("w_lo", [P, SLOTS, UNIT], F32R, r_wlo)
        xg_hi = place("xg_hi", [P, DC, TOK], F32R, r1)
        xg_lo = place("xg_lo", [P, DC, TOK], F32R, r2)
        x3 = place("x3", [P, NG, BLK, W], F32, r1)
        x3_hi = place("x3_hi", [P, DC, TOK], F32R, r2)
        pooled_hi = place("pooled_hi", [P, HC, TOK], F32R, r3)
        pooled_lo = place("pooled_lo", [P, HC, TOK], F32R, r3 + FULL // 2)
        merged = place("merged", [P, DC, TOK], F32, r3)
        x2 = place("x2", [P, NG, BLK, W], F32, r3)
        f_acc = place("f_acc", [P, NG, BLK, W], F32, r3)
        x3_lo = place("x3_lo", [P, DC, TOK], F32R, r3)
        x_nat = place("x_nat", [P, NG, BLK, W], F32, r4)
        r_pool = r4 + FULL - 3 * 4 * (PPAD + TOK) - 4 * TOK
        u_pool = place("u_pool", [P, PPAD + TOK], F32, r_pool)
        s_pool = place("s_pool", [P, 2, PPAD + TOK], F32, r_pool + 4 * (PPAD + TOK))
        pool_f = place("pool_f", [P, TOK], F32, r_pool + 12 * (PPAD + TOK))
        mixed_hi = place("mixed_hi", [P, HC, TOK], F32R, r4)
        mixed_lo = place("mixed_lo", [P, HC, TOK], F32R, r4 + FULL // 2)
        a_hi = place("a_hi", [P, HC, TOK], F32R, r4)
        a_lo = place("a_lo", [P, HC, TOK], F32R, r4 + FULL // 2)
        og = place("og", [P, NG, BLK, W], F32, r4)
        g_hi = place("g_hi", [P, 2, GRP, TOK], F32R, r4)
        g_lo = place("g_lo", [P, 2, GRP, TOK], F32R, r4 + FULL // 2)
        e_buf = place("e_buf", [P, NG, BLK, W], F32, r4)
        par_nat = place("par_nat", [P, 7, P], F32, r5)
        gain0_nat = place("gain0_nat", [DC, P], F32, r5 + 4096)
        squares_out = place("squares_out", [P, NG, W], F32, r5 + D * 4)
        a_conv = place("a_conv", [P, HC, PAD + TOK], F32, r5)
        gain_o = place("gain_o", [P, NG, W], F32, r5)
        up_gate = place("up_gate", [P, 2 + TOK], F32, r5)
        up_val = place("up_val", [P, 2 + TOK], F32, r5 + 2112)
        gate_c = place("gate_c", [P, TOK], F32, r5 + 4224)
        val_c = place("val_c", [P, TOK], F32, r5 + 6272)
        gelu_g = place("gelu_g", [P, TOK], F32, r5 + 8320)
        ff_prod = place("ff_prod", [P, TOK], F32, r5 + 10368)
        gain_f = place("gain_f", [P, NG, W], F32, r2 + FULL - 4 * D)
        p_nat = place("p_nat", [P, BLK, PLE], F32, r5)
        p_hi = place("p_hi", [P, PLEC, TOK], F32R, r5 + 4096)
        p_lo = place("p_lo", [P, PLEC, TOK], F32R, r5 + 8192)
        gain_e = place("gain_e", [P, NG, W], F32, r5)
        small = lambda name, shape: place(name, shape, F32, region(4 * int(np.prod(shape[1:]))))
        par = small("par", [P, C_ALL])
        ident = small("ident", [P, P])
        ones = small("ones", [P, P])
        diag = small("diag", [P, BLK, P])
        r_bc = small("r_bc", [P, TOK])
        sq = small("sq", [P, 2, TOK])
        acc = small("acc", [P, TOK])
        scaled = small("scaled", [P, TOK])
        sig = small("sig", [P, TOK])
        tmp = small("tmp", [P, TOK])
        conv_acc = small("conv_acc", [P, TOK])
        sums = small("sums", [P, BLK, NG])
        row_sum = small("row_sum", [P, BLK])
        std = small("std", [P, BLK])
        rstd = small("rstd", [P, BLK])
        eps = small("eps", [P, 1])
        inv_count = small("inv_count", [P, PPAD])
        assert cursor[0] <= nc.sbuf_usable_end, cursor[0]
        ps = ctx.enter_context(nc.psum_tensor("ps", [P, 8, TOK], F32))

        raw_in = [sem(f"raw_in{s}") for s in range(RAW)]
        slots_freed = sem("slots_freed")
        hi_ready, lo_ready, units_done = sem("hi_ready"), sem("lo_ready"), sem("units_done")
        tiles_taken, dve_chain = sem("tiles_taken"), sem("dve_chain")
        x_in = [sem(f"x_in{n}") for n in range(NG)]
        par_in0, par_in1 = sem("par_in0"), sem("par_in1")
        consts_ready, ident_zero = sem("consts_ready"), sem("ident_zero")
        par_turned, par_ready = sem("par_turned"), sem("par_ready")
        turned, turned_hi, turned_split = sem("turned"), sem("turned_hi"), sem("turned_split")
        row_squares, row_sums_ready, x2_ready, x3_ready = (sem(n) for n in ("row_squares", "row_sums_ready", "x2_ready", "x3_ready"))
        mean_sum_ready, sums_done, std_ready = sem("mean_sum_ready"), sem("sums_done"), sem("std_ready")
        diag_ready, spread_done = sem("diag_ready"), sem("spread_done")
        pool_f_ready, pooled_hi_ready, pooled_ready = sem("pool_f_ready"), sem("pooled_hi_ready"), sem("pooled_ready")
        mixed_hi_ready, mixed_rest_ready, sigmoid_ready = sem("mixed_hi_ready"), sem("mixed_rest_ready"), sem("sigmoid_ready")
        centred, squares_ready, squares_added = sem("centred"), sem("squares_ready"), sem("squares_added")
        ln_scaled, silu_ready, a_hi_ready, a_ready = (sem(n) for n in ("ln_scaled", "silu_ready", "a_hi_ready", "a_ready"))
        merged_ready, merged_hi_ready, merged_split = (sem(n) for n in ("merged_ready", "merged_hi_ready", "merged_split"))
        first_tap_ready, gate_conv_ready, gelu_ready = (sem(n) for n in ("first_tap_ready", "gate_conv_ready", "gelu_ready"))
        ff_ready, g_hi_ready, g_ready = sem("ff_ready"), sem("g_hi_ready"), sem("g_ready")
        ple_taken, y_ready = sem("ple_taken"), sem("y_ready")
        x_back, x2_out, f_zero, x2_in = (sem(n) for n in ("x_back", "x2_out", "f_zero", "x2_in"))
        gain_o_in, gain_f_in, gain_e_in = sem("gain_o_in"), sem("gain_f_in"), sem("gain_e_in")
        p_in, p_turned, p_hi_ready, p_ready = sem("p_in"), sem("p_turned"), sem("p_hi_ready"), sem("p_ready")
        out_done = sem("out_done")

        block = ctx.enter_context(nc.Block())

        @block.sync
        def _(sp):
            for_k = lambda w: w.rearrange("(k p) n -> p k n", p=P)
            win, wa, wb, wo = for_k(w_in), for_k(w_a_out), for_k(w_b_out), for_k(w_o)
            wup, wdn, wpg, wpl = for_k(w_up), for_k(w_down), for_k(w_ple_gate), for_k(w_ple)

            def load(u, src, width):
                if not (u.i is None and u.c < RAW):
                    sp.wait_ge(lo_ready, (u + (1 - RAW)).value())
                    sp.sem_inc(slots_freed, 1)
                s = u.slot(RAW)
                sp.dma_start(w_raw[:, s].rearrange("p (k n) -> p k n", n=width), src).then_inc(raw_in[s], 16)

            def half_column(u, w, col, h):
                load(u, w[:, 8 * h:8 * h + 8, bass.ds(col, P)], P)

            def column(u, w, col):
                for h in range(2):
                    half_column(u + h, w, col, h)

            def pair(u, w, cols):
                for h in range(2):
                    for j in range(2):
                        half_column(u + (2 * h + j), w, cols[j], h)

            def rows(u, w, k, n):
                load(u, w[:, bass.ds(k, 2), bass.ds(n * W, W)], W)

            xr = rows_of(x)
            for n in range(2):
                sp.dma_start(x_nat[:, n], xr[:, n]).then_inc(x_in[n], 16)
            for j in range(2):
                half_column(At(U_A + j), win, (H, 0)[j], 0)
            for n in range(2, NG):
                sp.dma_start(x_nat[:, n], xr[:, n]).then_inc(x_in[n], 16)
            for j in range(2):
                half_column(At(U_A + 2 + j), win, (H, 0)[j], 1)
            with sp.Fori(1, HC) as c:
                column(At(U_A, c, 4), win, c * P + H)
                column(At(U_A + 2, c, 4), win, c * P)
            with sp.Fori(0, HC) as c:
                column(At(U_B, c, 2), win, c * P + 2 * H)
            column(At(U_M1 - 2), win, 3 * H + D)
            pw = pool_w.rearrange("g (k p) d -> p (g k) d", p=P)
            for n in range(2):
                load(At(U_M1 + n), pw[:, 4 * n:4 * n + 4, :], PGD)
            half_column(At(U_M1 + 2), wb, 0, 0)
            column(At(U_M1 + 3), win, 3 * H + D + P)
            half_column(At(U_M1 + 5), wb, P, 0)
            for first, start, w, gates in ((U_M1, 1, wb, 3 * H + D), (U_M2, 0, wa, 3 * H)):
                with sp.Fori(start, DC // 2) as m2:
                    for j in range(2):
                        column(At(first + 3 * j, m2, 6), win, m2 * (2 * P) + (gates + j * P))
                        half_column(At(first + 3 * j + 2, m2, 6), w, m2 * (2 * P) + j * P, 0)
            with sp.Fori(0, NG) as n:
                for v in range(DC // 2):
                    rows(At(U_O + v, n, 8), wo, 2 * v, n)
            pair(At(F_UP(0)), wup, (0, FF))
            with sp.Fori(1, GRP) as c:
                column(At(F_UP(0), c, 4), wup, c * P)
                column(At(F_UP(0) + 2, c, 4), wup, c * P + FF)
            with sp.Fori(0, NGRP - 1) as j:
                for c in range(GRP):
                    column(At(F_UP(1) + 4 * c, j, 24), wup, j * (GRP * P) + (GRP + c) * P)
                    column(At(F_UP(1) + 4 * c + 2, j, 24), wup, j * (GRP * P) + ((GRP + c) * P + FF))
                for n in range(NG):
                    for v in range(GRP // 2):
                        rows(At(F_DOWN(0) + 2 * n + v, j, 24), wdn, j * GRP + 2 * v, n)
            with sp.Fori(0, NG) as n:
                for v in range(GRP // 2):
                    rows(At(F_DOWN(NGRP - 1) + v, n, 2), wdn, (NGRP - 1) * GRP + 2 * v, n)
            for n in range(NG):
                rows(At(U_L + n), wpl, 0, n)
            with sp.Fori(0, NG) as n:
                for v in range(DC // 2):
                    rows(At(U_G + v, n, 8), wpg, 2 * v, n)
            for n in range(NG):
                sp.wait_ge(y_ready, BLK * (n + 1))
                sp.dma_start(rows_of(out)[:, n], e_buf[:, n]).then_inc(out_done, 16)
            sp.wait_ge(out_done, 16 * NG)

        @block.gpsimd
        def _(pool):
            on_all = lambda g: g.partition_broadcast(P).rearrange("p (n f) -> p n f", f=W)
            nc.gpsimd.memset(ident[:], 0.0).then_inc(ident_zero, 1)
            pool.wait_ge(ident_zero, 1)
            nc.gpsimd.affine_select(out=ident[:], in_=ident[:], compare_op=ALU.not_equal, fill=1.0, base=0,
                                    pattern=[[-1, P]], channel_multiplier=1).then_inc(consts_ready, 1)
            nc.gpsimd.memset(ones[:], 1.0).then_inc(consts_ready, 1)
            nc.gpsimd.memset(eps[:], EPS).then_inc(consts_ready, 1)
            for t in range(PPAD):
                nc.gpsimd.memset(inv_count[:, t:t + 1], 1.0 / (t + 1)).then_inc(consts_ready, 1)
            pool.wait_ge(ln_scaled, HC)
            pool.dma_start(gain_o[:], on_all(mix_post_g)).then_inc(gain_o_in, 16)
            pool.wait_ge(x2_ready, NG * BLK)
            pool.dma_start(x2_dram, x2[:]).then_inc(x2_out, 16)
            pool.wait_ge(x2_out, 16)
            pool.wait_ge(row_squares, 2 * BLK)
            pool.wait_ge(turned, 2 * DC)
            nc.gpsimd.memset(f_acc[:], 0.0).then_inc(f_zero, 1)
            pool.wait_ge(units_done, F_UP(NGRP - 1) + 4 * GRP)
            pool.dma_start(gain_f[:], on_all(ffn_post_g)).then_inc(gain_f_in, 16)
            pool.dma_start(x3[:], x2_dram).then_inc(x2_in, 16)
            pool.wait_ge(g_ready, FC)
            pool.dma_start(p_nat[:], p.rearrange("z a (b t) d -> t (z a b) d", t=P)).then_inc(p_in, 16)
            pool.wait_ge(units_done, U_G)
            pool.dma_start(gain_e[:], on_all(ple_post_g)).then_inc(gain_e_in, 16)

        @block.tensor
        def _(pe):
            pe.wait_ge(consts_ready, 2)

            def bank_free(t, banks):
                if not (t.i is None and t.c < banks):
                    pe.wait_ge(tiles_taken, (t + (1 - banks)).value())

            def products(o, s, cols, hi, lo, start, stop):
                pe.matmul(o, w_hi[:, s, cols], hi, start=start, stop=False)
                pe.matmul(o, w_hi[:, s, cols], lo, start=False, stop=False)
                return pe.matmul(o, w_lo[:, s, cols], hi, start=False, stop=stop)

            def chunk_products(o, u, k, hi, lo, chunks):
                last = products(o, u.slot(SLOTS), slice(k % 8 * P, (k % 8 + 1) * P), hi[:, k], lo[:, k], k == 0, k == chunks - 1)
                if k % 8 == 7:
                    last.then_inc(units_done, 1)

            def tile(u, t, hi, lo, chunks=DC, arrives=None, bank=None, banks=4, between=None):
                bank_free(t, banks)
                for k in range(chunks):
                    if k % 8 == 0:
                        if k and between:
                            between()
                        pe.wait_ge(lo_ready, (u + (k // 8 + 1)).value())
                    if arrives is not None:
                        pe.wait_ge(arrives, k + 1)
                    chunk_products(ps[:, t.slot(4) if bank is None else bank], u + k // 8, k, hi, lo, chunks)

            def turn(src, base, c, bank0):
                if c >= BLK:
                    pe.wait_ge(turned_split, base + c - 3)
                n, q = c // 4, c % 4
                for b in range(BLK):
                    mm = pe.transpose(ps[:, bank0 + q, b * P:(b + 1) * P], src[:, n, b, q * P:(q + 1) * P], ident[:])
                mm.then_inc(turned, 1)

            def first_pair(u, src, base, arrived, tile_bank, turn_bank):
                def turns(n):
                    if n < NG:
                        arrived(n)
                        for c in range(4 * n, 4 * n + 4):
                            turn(src, base, c, turn_bank)
                turns(0)
                for k in range(DC):
                    if k % 4 == 0:
                        turns(k // 4 + 1)
                    pe.wait_ge(turned_split, base + k + 1)
                    for j in range(2):
                        if k % 8 == 0:
                            pe.wait_ge(lo_ready, u + 2 * (k // 8) + j + 1)
                        chunk_products(ps[:, tile_bank + j], At(u + 2 * (k // 8) + j), k, xg_hi, xg_lo, DC)

            def rows(u, t, bank0, x_hi, x_lo, chunks, wait=None, ahead=None):
                for v in range(chunks // 2):
                    if ahead is not None:
                        ahead(v)
                    pe.wait_ge(lo_ready, (u + (v + 1)).value())
                    for b in range(BLK):
                        if v == 0 and t is not None:
                            bank_free(t + b, 8)
                        if wait is not None and b == 0:
                            pe.wait_ge(wait[0], wait[1] + 2 * v + 2)
                        for kk in range(2):
                            k, o = 2 * v + kk, ps[:, bank0 + b]
                            cols, tok, s = slice(kk * W, (kk + 1) * W), slice(b * P, (b + 1) * P), (u + v).slot(SLOTS)
                            pe.matmul(o, x_hi[:, k, tok], w_hi[:, s, cols], start=k == 0, stop=False)
                            pe.matmul(o, x_lo[:, k, tok], w_hi[:, s, cols], start=False, stop=False)
                            last = pe.matmul(o, x_hi[:, k, tok], w_lo[:, s, cols], start=False, stop=k == chunks - 1)
                    last.then_inc(units_done, 1)

            def spread(n, bank):
                pe.wait_ge(diag_ready, n)
                for b in range(BLK):
                    mm = pe.matmul(ps[:, bank, b * P:(b + 1) * P], ones[:], diag[:, b], start=True, stop=True)
                mm.then_inc(spread_done, 1)

            pe.wait_ge(par_in0, 16)
            pe.transpose(ps[:, 2, 0:DC], gain0_nat[:], ident[0:DC, 0:DC]).then_inc(par_turned, 1)
            first_pair(U_A, x_nat, 0, lambda n: pe.wait_ge(x_in[n], 16), 0, 4)
            pe.wait_ge(par_in1, 16 * 12)
            pe.wait_ge(par_ready, 1)
            n = CONV_W * HC // 2
            pe.transpose(ps[:, 2, 0:C_CAW], par_nat[0:C_CAW, 0], ident[0:C_CAW, 0:C_CAW])
            for j in range(2):
                pe.transpose(ps[:, 2, C_CAW + j * n:C_CAW + (j + 1) * n], par_nat[0:n, 1 + j], ident[0:n, 0:n])
            n = 2 * FC
            for j in range(1 + FTAPS):
                mm = pe.transpose(ps[:, 3, j * n:(j + 1) * n], par_nat[0:n, 3 + j], ident[0:n, 0:n])
            mm.then_inc(par_turned, 1)
            spread(1, 7)
            pe.wait_ge(par_ready, 2)
            for j in range(2, 4):
                tile(At(U_A + 2 * j), At(T_A + j), xg_hi, xg_lo)
            with pe.Fori(1, HC // 2) as i:
                for j in range(4):
                    tile(At(U_A + 2 * j, i, 8), At(T_A + j, i, 4), xg_hi, xg_lo)
            with pe.Fori(0, 2) as i:
                for j in range(4):
                    tile(At(U_B + 2 * j, i, 8), At(T_B + j, i, 4), xg_hi, xg_lo)
            tile(At(U_M1 - 2), At(T_M1 - 4), xg_hi, xg_lo)
            for n in range(2):
                u = At(U_M1 + n)
                pe.wait_ge(lo_ready, (u + 1).value())
                for j in range(4):
                    g, mo = 2 * n + j // 2, j % 2
                    if n == 0:
                        bank_free(At(T_M1 - 3 + j), 4)
                    pe.wait_ge(pooled_ready, 2 * g + 2)
                    for k in range(2):
                        at = (2 * (j // 2) + k) * PGD + mo * P
                        last = products(ps[:, (T_M1 + 1 + j) % 4 if n == 0 else 4 + j], u.slot(SLOTS), slice(at, at + P),
                                        pooled_hi[:, 2 * g + k], pooled_lo[:, 2 * g + k], k == 0, k == 1)
                last.then_inc(units_done, 1)
            pe.wait_ge(tiles_taken, T_M1 + 1)
            pe.wait_ge(mixed_rest_ready, 4)

            def branch(u, t, hi, lo, arrives=None, ahead_of_branch=None, within_gate=None, gate=True):
                if gate:
                    tile(u, t, xg_hi, xg_lo, between=within_gate)
                if ahead_of_branch:
                    ahead_of_branch()
                tile(u + 2, t + 1, hi, lo, chunks=HC, arrives=arrives)

            for m in range(4):
                branch(At(U_M1 + 3 * m), At(T_M1 + 2 * m), mixed_hi, mixed_lo, gate=m > 0)
            with pe.Fori(1, 3) as i:
                for j in range(4):
                    branch(At(U_M1 + 3 * j, i, 12), At(T_M1 + 2 * j, i, 8), mixed_hi, mixed_lo)

            def mean():
                pe.wait_ge(mean_sum_ready, 1)
                pe.matmul(ps[:, 7], ones[:], acc[:], start=True, stop=True).then_inc(spread_done, 1)

            for m in range(12, DC):
                branch(At(U_M1 + 3 * m), At(T_M1 + 2 * m), mixed_hi, mixed_lo, ahead_of_branch=mean if m == 12 else None)

            def variance():
                pe.wait_ge(squares_added, HC)
                for b in range(BLK):
                    mm = pe.matmul(ps[:, 4, b:b + 1], acc[:, b * P:(b + 1) * P], ones[:, 0:1], start=True, stop=True)
                mm.then_inc(sums_done, 1)
                spread(2, 7)

            for m in range(4):
                branch(At(U_M2 + 3 * m), At(T_M2 + 2 * m), a_hi, a_lo, arrives=a_ready if m == 0 else None,
                       within_gate=variance if m == 0 else None)
            with pe.Fori(1, DC // 4) as i:
                for j in range(4):
                    branch(At(U_M2 + 3 * j, i, 12), At(T_M2 + 2 * j, i, 8), a_hi, a_lo)
            pe.wait_ge(tiles_taken, T_O)
            with pe.Fori(0, NG // 2) as i:
                for n in range(2):
                    rows(At(U_O + 8 * n, i, 16), At(T_O + 4 * n, i, 8), 4 * n, xg_hi, xg_lo, DC, wait=(merged_split, 0))

            first_pair(U_F, x2, DC, lambda n: pe.wait_ge(x2_ready, BLK * (n + 1)), 4, 0)
            spread(3, 3)

            def up(u, t, first=False):
                for w in range(2 if first else 0, 2 * GRP):
                    if first and w == 2 * GRP - 1:
                        pe.wait_ge(tiles_taken, T_F + 1)
                    tile(u + 2 * w, t + w, xg_hi, xg_lo, bank=(w + 4) % 8, banks=8)

            def down(u, t, half):
                for n in range(NG):
                    rows(u + 2 * n, t + 4 * n, 4 * ((n + 1) % 2), g_hi[:, half], g_lo[:, half], GRP)

            up(At(F_UP(0)), At(FT_UP(0)), first=True)
            with pe.Fori(0, (NGRP - 1) // 2) as i:
                for s in range(2):
                    up(At(F_UP(1 + s), i, 48), At(FT_UP(1 + s), i, 48))
                    pe.wait_ge(g_ready, At(GRP * (1 + s), i, 2 * GRP).value())
                    down(At(F_DOWN(s), i, 48), At(FT_DOWN(s), i, 48), s)
            pe.wait_ge(g_ready, FC)
            pe.wait_ge(p_in, 16)
            pe.wait_ge(tiles_taken, FT_DOWN(NGRP - 1))
            for k in range(PLEC):
                for b in range(BLK):
                    mm = pe.transpose(ps[:, k, b * P:(b + 1) * P], p_nat[:, b, k * P:(k + 1) * P], ident[:])
            mm.then_inc(p_turned, 1)
            pe.wait_ge(p_ready, PLEC)
            down(At(F_DOWN(NGRP - 1)), At(FT_DOWN(NGRP - 1)), 0)
            for n in range(NG):
                if n == 0:
                    pe.wait_ge(tiles_taken, T_G - 4)
                elif n == 1:
                    pe.wait_ge(tiles_taken, T_G)
                else:
                    pe.wait_ge(ple_taken, 4 * (n - 1))
                rows(At(U_L + n), None, 4 * ((n + 1) % 2), p_hi, p_lo, PLEC)
            pe.wait_ge(ple_taken, DC)

            def turns(v):
                for n in {0: (0, 1), 2: (2,), 4: (3,)}.get(v, ()):
                    pe.wait_ge(x3_ready, BLK * (n + 1))
                    for c in range(4 * n, 4 * n + 4):
                        turn(x3, 2 * DC, c, 0)

            for n in range(NG):
                if n == 1:
                    pe.wait_ge(turned_split, 3 * DC)
                rows(At(U_G + 8 * n), At(T_G + 4 * n) if n > 1 else None, 4 * ((n + 1) % 2), x3_hi, x3_lo, DC,
                     wait=(turned_split, 2 * DC) if n == 0 else None, ahead=turns if n == 0 else None)

        @block.scalar
        def _(act):
            f = act.activation

            def split(u):
                act.wait_ge(raw_in[u.slot(RAW)], u.raw_count().value())
                f(w_hi[:, u.slot(SLOTS)], w_raw[:, u.slot(RAW)], ACT.Copy).then_inc(hi_ready, 1)

            def step(u, ahead=True):
                act.wait_ge(units_done, (u + 1).value())
                if ahead:
                    split(u + SLOTS)

            def standard_deviation(total, src):
                f(std[:], src, ACT.Sqrt, bias=eps[:], scale=1.0 / total).then_inc(std_ready, 1)

            def row_squares_of(src, done):
                for b in range(BLK):
                    if done + b > 0:
                        act.wait_ge(row_squares, done + b)
                    f(squares_out[:], src[:, :, b], ACT.Square, accum_out=row_sum[:, b:b + 1]).then_inc(row_squares, 1)
                act.wait_ge(row_squares, done + BLK)

            def turned_high(base, c, bank0, dst, scale):
                act.wait_ge(turned, base + c + 1)
                f(dst[:, c], ps[:, bank0 + c % 4], ACT.Identity, scale=scale).then_inc(turned_hi, 1)

            def tile_squares(src, b, n, k):
                act.wait_ge(squares_ready, k)
                f(sq[:, 0], src, ACT.Square, accum_out=sums[:, b, n:n + 1]).then_inc(squares_ready, 1)

            def param(base, q):
                return par[:, q.c + base:q.c + base + 1] if q.i is None else par[:, bass.ds(q.i * q.k + (q.c + base), 1)]

            as_rows = lambda v: v.rearrange("(c p) -> c p", p=P)
            act.dma_start(gain0_nat[:], as_rows(mix_pre_g)).then_inc(par_in0, 16)
            act.wait_ge(x_in[1], 16)
            for col, v in ((C_FFNPRE, ffn_pre_g), (C_CAB, conv_a_b), (C_LNG, ln_a_g), (C_LNB, ln_a_b), (C_PSC, pool_scale)):
                act.dma_start(par_nat[col:col + v.shape[0] // P, 0], as_rows(v)).then_inc(par_in1, 16)
            act.dma_start(par_nat[0:DC, 0], as_rows(mix_pre_g)).then_inc(par_in1, 16)
            taps = conv_a_w.rearrange("k (c p) -> (k c) p", p=P)
            n = CONV_W * HC // 2
            for j in range(2):
                act.dma_start(par_nat[0:n, 1 + j], taps[j * n:(j + 1) * n]).then_inc(par_in1, 16)
            act.dma_start(par_nat[0:2 * FC, 3], as_rows(conv_f_b)).then_inc(par_in1, 16)
            for k in range(FTAPS):
                act.dma_start(par_nat[0:2 * FC, 4 + k], as_rows(conv_f_w[k])).then_inc(par_in1, 16)

            act.wait_ge(par_ready, 1)
            for c in range(DC):
                turned_high(0, c, 4, xg_hi, par[:, C_MIXPRE + c:C_MIXPRE + c + 1])
                if c in (3, 5, 7, 9):
                    split(At((c - 3) // 2))
            for k in range(2):
                step(At(U_A + k))
            act.wait_ge(consts_ready, 3)
            row_squares_of(x_nat, 0)
            standard_deviation(D, row_sum[:])

            def sigmoid(t):
                act.wait_ge(tiles_taken, (t + 1).value())
                f(sig[:], scaled[:], ACT.Sigmoid).then_inc(sigmoid_ready, 1)

            for k in range(2, 4):
                step(At(U_A + k))
            sigmoid(At(T_A))

            def glu(u, t):
                step(u)
                step(u + 1)
                sigmoid(t)
                step(u + 2)
                step(u + 3)

            glu(At(U_A + 4), At(T_A + 2))
            with act.Fori(1, HC // 2) as i:
                for j in range(2):
                    glu(At(U_A + 4 * j, i, 8), At(T_A + 2 * j, i, 4))
            for c in range(HC):
                step(At(U_B + 2 * c))
                step(At(U_B + 2 * c + 1))
                act.wait_ge(pool_f_ready, c + 1)
                f(pooled_hi[:, c], pool_f[:], ACT.Copy).then_inc(pooled_hi_ready, 1)

            def branch(u, t, within_gate=None):
                step(u)
                if within_gate:
                    within_gate()
                step(u + 1)
                sigmoid(t)
                step(u + 2)

            step(At(U_M1 - 2))
            step(At(U_M1 - 1))
            sigmoid(At(T_M1 - 4))
            for n in range(2):
                step(At(U_M1 + n))
                for j in range(4):
                    c = 4 * n + j
                    f(mixed_hi[:, c], ps[:, (T_M1 + 1 + j) % 4 if n == 0 else 4 + j], ACT.Identity,
                      scale=par[:, C_PSC + c:C_PSC + c + 1]).then_inc(mixed_hi_ready, 1)
            step(At(U_M1 + 2))
            for m in range(1, 4):
                branch(At(U_M1 + 3 * m), At(T_M1 + 2 * m))
            with act.Fori(1, 3) as i:
                for j in range(4):
                    branch(At(U_M1 + 3 * j, i, 12), At(T_M1 + 2 * j, i, 8))

            def centred_squares(c):
                act.wait_ge(centred, c + 1)
                if c >= 2:
                    act.wait_ge(squares_added, c - 1)
                f(sq[:, c % 2], a_conv[:, c, PAD:], ACT.Square).then_inc(squares_ready, 1)

            for j in range(4):
                u, t = At(U_M1 + 36 + 3 * j), At(T_M1 + 24 + 2 * j)
                branch(u, t)
                for c in (2 * j, 2 * j + 1):
                    centred_squares(c)

            def layer_norm():
                act.wait_ge(sums_done, 1)
                standard_deviation(H, ps[:, 4, 0:BLK])
                for c in range(HC):
                    act.wait_ge(ln_scaled, c + 1)
                    if c > 0:
                        act.wait_ge(a_ready, c)
                    f(tmp[:], (scaled, conv_acc)[c % 2][:], ACT.Silu, bias=par[:, C_LNB + c:C_LNB + c + 1]).then_inc(silu_ready, 1)
                    act.wait_ge(silu_ready, c + 1)
                    f(a_hi[:, c], tmp[:], ACT.Copy).then_inc(a_hi_ready, 1)

            branch(At(U_M2), At(T_M2), within_gate=layer_norm)
            for m in range(1, 4):
                branch(At(U_M2 + 3 * m), At(T_M2 + 2 * m))
            with act.Fori(1, DC // 4) as i:
                for j in range(4):
                    branch(At(U_M2 + 3 * j, i, 12), At(T_M2 + 2 * j, i, 8))
            for c in range(DC):
                act.wait_ge(merged_ready, c + 1)
                f(xg_hi[:, c], merged[:, c], ACT.Copy).then_inc(merged_hi_ready, 1)
            act.wait_ge(merged_split, DC)
            for n in range(NG):
                act.dma_start(x2[:, n], rows_of(x)[:, n]).then_inc(x_back, 16)

            for n in range(NG):
                for v in range(DC // 2):
                    step(At(U_O + 8 * n + v))
                for b in range(BLK):
                    tile_squares(ps[:, 4 * (n % 2) + b], b, n, Q_O + 4 * n + b)
            act.wait_ge(row_sums_ready, 1)
            standard_deviation(D, row_sum[:])
            for c in range(DC):
                turned_high(DC, c, 0, xg_hi, par[:, C_FFNPRE + c:C_FFNPRE + c + 1])
                if c == 11:
                    step(At(U_F))
                    step(At(U_F + 1))
            row_squares_of(x2, BLK)
            standard_deviation(D, row_sum[:])

            def up(u, t, q, half, first=False):
                def high(c):
                    act.wait_ge(ff_ready, (q + (c + 1)).value())
                    f(g_hi[:, half, c], ff_prod[:], ACT.Copy).then_inc(g_hi_ready, 1)

                def first_tap(dst, src, c, j):
                    act.wait_ge(tiles_taken, (t + (2 * c + j + 1)).value())
                    f(dst[:], src[:, 0:TOK], ACT.Identity, scale=param(C_CFW + j * FC, q + c),
                      bias=param(C_CFB + j * FC, q + c)).then_inc(first_tap_ready, 1)

                def gelu(c):
                    act.wait_ge(gate_conv_ready, (q + (c + 1)).value())
                    f(gelu_g[:], gate_c[:], ACT.Gelu_apprx_tanh).then_inc(gelu_ready, 1)

                for c in range(GRP):
                    if first and c == 0:
                        step(u + 2)
                        step(u + 3)
                        first_tap(gate_c, up_gate, c, 0)
                        gelu(c)
                    else:
                        step(u + 4 * c)
                        if c > 0:
                            high(c - 1)
                        step(u + (4 * c + 1))
                        first_tap(gate_c, up_gate, c, 0)
                        step(u + (4 * c + 2))
                        gelu(c)
                        step(u + (4 * c + 3))
                    first_tap(val_c, up_val, c, 1)
                high(GRP - 1)

            up(At(F_UP(0)), At(FT_UP(0)), At(0), 0, first=True)
            with act.Fori(0, (NGRP - 1) // 2) as i:
                for s in range(2):
                    up(At(F_UP(1 + s), i, 48), At(FT_UP(1 + s), i, 48), At(GRP * (1 + s), i, 2 * GRP), 1 - s)
                    for v in range(2 * NG):
                        step(At(F_DOWN(s) + v, i, 48))
            act.wait_ge(p_turned, 1)
            for k in range(PLEC):
                f(p_hi[:, k], ps[:, k], ACT.Copy).then_inc(p_hi_ready, 1)
            for n in range(NG):
                for v in range(2):
                    step(At(F_DOWN(NGRP - 1) + 2 * n + v))
                for b in range(BLK):
                    act.wait_ge(tiles_taken, FT_DOWN(NGRP - 1) + 4 * n + b + 1)
                    tile_squares(f_acc[:, n, b], b, n, Q_F + 4 * n + b)
            act.wait_ge(row_sums_ready, 2)
            standard_deviation(D, row_sum[:])
            for n in range(NG):
                step(At(U_L + n))
                for b in range(BLK):
                    f(e_buf[:, n, b], ps[:, 4 * ((n + 1) % 2) + b], ACT.Copy).then_inc(ple_taken, 1)
            for c in range(DC):
                turned_high(2 * DC, c, 0, x3_hi, 1.0)
                if c % 4 == 3 and c > 4:
                    step(At(U_G + c // 4 - 1))
            for n in range(NG):
                for v in range(3 if n == 0 else 0, DC // 2):
                    u = U_G + 8 * n + v
                    step(At(u), ahead=u + SLOTS < U_END)
                for b in range(BLK):
                    if 4 * n + b >= 2:
                        act.wait_ge(tiles_taken, T_G + 4 * n + b - 1)
                    f((sig, scaled)[b % 2][:], ps[:, 4 * ((n + 1) % 2) + b], ACT.Sigmoid).then_inc(sigmoid_ready, 1)
                for b in range(BLK):
                    act.wait_ge(tiles_taken, T_G + 4 * n + b + 1)
                    tile_squares(e_buf[:, n, b], b, n, Q_E + 4 * n + b)
            act.wait_ge(row_sums_ready, 3)
            standard_deviation(D, row_sum[:])

        @block.vector
        def _(dve):
            op = Tally(dve, dve_chain)
            as_f32 = lambda ap: ap.bitcast(F32)
            flat = lambda ap: ap.rearrange("p a t -> p (a t)")

            def step(u):
                split(u + SLOTS)

            def split(u):
                dve.wait_ge(hi_ready, (u + 1).value())
                s = u.slot(SLOTS)
                dve.tensor_tensor(w_lo[:, s], w_raw[:, u.slot(RAW)], as_f32(w_hi[:, s]), ALU.subtract).then_inc(lo_ready, 1)

            def scale_tile(dst, t, bank=None):
                dve.tensor_tensor(dst, ps[:, t.slot(4) if bank is None else bank], r_bc[:], ALU.mult).then_inc(tiles_taken, 1)

            def token_factors(n):
                dve.wait_ge(std_ready, n)
                op(dve.reciprocal(rstd[:], std[:]))
                op.settle()

            def factors_on_all(n, k, bank, dst):
                for b in range(BLK):
                    ins = dve.tensor_scalar(diag[:, b], ident[:], rstd[:, b:b + 1], None, ALU.mult)
                ins.then_inc(diag_ready, 1)
                dve.wait_ge(spread_done, k)
                op(dve.tensor_copy(dst[:], ps[:, bank]))
                op.settle()

            def low(dst, src, hi, done):
                dve.tensor_tensor(dst, src, as_f32(hi), ALU.subtract).then_inc(done, 1)

            def scaled_low(dst, src, scale, hi, done):
                dve.scalar_tensor_tensor(out=dst, in0=src, scalar=scale, in1=as_f32(hi), op0=ALU.mult, op1=ALU.subtract).then_inc(done, 1)

            def add_rows(dst, src, b, base, done):
                dve.scalar_tensor_tensor(out=dst, in0=src, scalar=rstd[:, b:b + 1], in1=base, op0=ALU.mult, op1=ALU.add).then_inc(done, 1)

            def sum_groups(squares):
                dve.wait_ge(squares_ready, squares)
                dve.tensor_reduce(row_sum[:], sums[:], AX.X, ALU.add).then_inc(row_sums_ready, 1)

            def param(base, q):
                return par[:, q.c + base:q.c + base + 1] if q.i is None else par[:, bass.ds(q.i * q.k + (q.c + base), 1)]

            dve.wait_ge(par_turned, 1)
            dve.tensor_copy(par[:, 0:DC], ps[:, 2, 0:DC]).then_inc(par_ready, 1)
            dve.wait_ge(par_ready, 1)
            for c in range(DC):
                dve.wait_ge(turned_hi, c + 1)
                scaled_low(xg_lo[:, c], ps[:, 4 + c % 4], param(C_MIXPRE, At(c)), xg_hi[:, c], turned_split)
                if c in (3, 5, 7, 9):
                    split(At((c - 3) // 2))
            for k in range(2):
                step(At(U_A + k))
            dve.wait_ge(par_turned, 2)
            op(dve.tensor_copy(par[:, DC:C_CFB], ps[:, 2, DC:C_CFB]))
            dve.tensor_copy(par[:, C_CFB:C_ALL], ps[:, 3, 0:C_ALL - C_CFB]).then_inc(par_ready, 1)
            dve.wait_ge(par_ready, 2)
            dve.wait_ge(consts_ready, 3 + PPAD)
            token_factors(1)
            factors_on_all(1, 1, 7, r_bc)

            op(dve.memset(a_conv[:, :, 0:PAD], 0.0))
            op(dve.memset(acc[:], 0.0))
            op.settle()

            def conv_taps(c, first, last):
                chunk = lambda k: flat(a_conv[:, bass.ds(c, 1), k:k + TOK])
                both = (conv_acc[:], sq[:, 1])
                for k in range(first, last):
                    weight = par[:, bass.ds(c + (C_CAW + k * HC), 1)]
                    op.settle(but=1 if k > 0 else 0)
                    if k == 0:
                        op(dve.tensor_scalar(both[0], chunk(0), weight, par[:, bass.ds(c + C_CAB, 1)], ALU.mult, ALU.add))
                    elif k == 1:
                        op(dve.tensor_scalar(both[1], chunk(1), weight, None, ALU.mult))
                    else:
                        op(dve.scalar_tensor_tensor(out=both[k % 2], in0=chunk(k), scalar=weight, in1=both[k % 2],
                                                    op0=ALU.mult, op1=ALU.add))
                if last == CONV_W:
                    op.settle()
                    op(dve.tensor_tensor(chunk(PAD), both[0], both[1], ALU.add))
                    op.settle()
                    op(dve.tensor_tensor(acc[:], acc[:], chunk(PAD), ALU.add))

            def glu_product(dst, t, sigmoids):
                scale_tile(tmp[:], t)
                dve.wait_ge(tiles_taken, (t + 1).value())
                dve.wait_ge(sigmoid_ready, sigmoids.value())
                op(dve.tensor_tensor(dst, tmp[:], sig[:], ALU.mult))

            def glu_chunks(i, js):
                for j in js:
                    taps = ((7, 13), (13, 19), (19, 26), (26, CONV_W)) if j == 1 else ((0, 0), (0, 0), (0, 0), (0, 7))
                    straight = isinstance(i, int)
                    at = lambda first, k: At(first + i * k) if straight else At(first, i, k)
                    u, t = at(U_A + 4 * j, 8), at(T_A + 2 * j, 4)
                    if straight and j == 0:
                        step(u + 2)
                        step(u + 3)
                        scale_tile(scaled[:], t)
                    else:
                        step(u)
                        conv_taps(i, *taps[0])
                        step(u + 1)
                        scale_tile(scaled[:], t)
                        conv_taps(i, *taps[1])
                        step(u + 2)
                        conv_taps(i, *taps[2])
                        step(u + 3)
                    glu_product(flat(a_conv[:, bass.ds(i * 2 + j, 1), PAD:]), t + 1, at(G_A + j + 1, 2))
                    conv_taps(i, *taps[3])

            glu_chunks(0, (0, 1))
            per = 2 + CONV_W + 2
            with dve.Fori(1, HC // 2) as i:
                op.enter(i, per, start=1)
                glu_chunks(i, (0, 1))
            op.leave(HC // 2, per, start=1)

            op(dve.memset(u_pool[:, 0:PPAD], 0.0))

            def pooled_low(c):
                dve.wait_ge(pooled_hi_ready, c + 1)
                low(pooled_lo[:, c], pool_f[:], pooled_hi[:, c], pooled_ready)

            TAPS_B = (0, 6, 12, 17, 22, 25, 28, 30, CONV_W)
            for c in range(HC):
                w = WINDOWS[c // 2]
                step(At(U_B + 2 * c))
                if c > 0:
                    pooled_low(c - 1)
                conv_taps(HC // 2, TAPS_B[c], TAPS_B[c + 1])
                step(At(U_B + 2 * c + 1))
                scale_tile(u_pool[:, PPAD:], At(T_B + c))
                dve.wait_ge(tiles_taken, T_B + c + 1)
                have, s = 1, u_pool
                while have < w:
                    dst = s_pool[:, have.bit_length() % 2]
                    op.settle()
                    op(dve.tensor_tensor(dst[:, 2 * have - 1:], s[:, 2 * have - 1:], s[:, have - 1:PPAD + TOK - have], ALU.add))
                    s, have = dst, 2 * have
                op.settle()
                op(dve.tensor_tensor(pool_f[:, 0:w - 1], s[:, PPAD:PPAD + w - 1], inv_count[:, 0:w - 1], ALU.mult))
                op.settle()
                op(dve.tensor_tensor(pool_f[:, 0:w - 1], pool_f[:, 0:w - 1], u_pool[:, PPAD:PPAD + w - 1], ALU.subtract))
                dve.scalar_tensor_tensor(out=pool_f[:, w - 1:], in0=s[:, PPAD + w - 1:], scalar=1.0 / w,
                                         in1=u_pool[:, PPAD + w - 1:], op0=ALU.mult, op1=ALU.subtract).then_inc(pool_f_ready, 1)
                dve.wait_ge(pool_f_ready, c + 1)

            def gated(dst, t, sigmoids, done):
                dve.wait_ge(sigmoid_ready, sigmoids.value())
                dve.tensor_tensor(dst, ps[:, t.slot(4)], sig[:], ALU.mult).then_inc(done, 1)

            def m1_taps(j):
                return ((8 * j, 8 * j + 3), (8 * j + 3, 8 * j + 5), (8 * j + 5, min(8 * j + 8, CONV_W)))

            step(At(U_M1 - 2))
            pooled_low(HC - 1)
            step(At(U_M1 - 1))
            scale_tile(scaled[:], At(T_M1 - 4))
            for n in range(2):
                step(At(U_M1 + n))
                for j in range(4):
                    c = 4 * n + j
                    dve.wait_ge(mixed_hi_ready, c + 1)
                    scaled_low(mixed_lo[:, c], ps[:, (T_M1 + 1 + j) % 4 if n == 0 else 4 + j], param(C_PSC, At(c)),
                               mixed_hi[:, c], tiles_taken if n == 0 else mixed_rest_ready)
            step(At(U_M1 + 2))
            gated(merged[:, 0], At(T_M1 + 1), At(G_M1 + 1), tiles_taken)
            conv_taps(HC // 2 + 1, 0, 8)
            for j in range(1, 4):
                u, t, taps = At(U_M1 + 3 * j), At(T_M1 + 2 * j), m1_taps(j)
                step(u)
                conv_taps(HC // 2 + 1, *taps[0])
                step(u + 1)
                scale_tile(scaled[:], t)
                conv_taps(HC // 2 + 1, *taps[1])
                step(u + 2)
                gated(merged[:, j], t + 1, At(G_M1 + j + 1), tiles_taken)
                conv_taps(HC // 2 + 1, *taps[2])
            per = CONV_W + 2
            with dve.Fori(1, 3) as i:
                op.enter(i, per, start=1)
                for j in range(4):
                    c, taps = i + (HC // 2 + 1), m1_taps(j)
                    u, t = At(U_M1 + 3 * j, i, 12), At(T_M1 + 2 * j, i, 8)
                    step(u)
                    conv_taps(c, *taps[0])
                    step(u + 1)
                    scale_tile(scaled[:], t)
                    conv_taps(c, *taps[1])
                    step(u + 2)
                    gated(flat(merged[:, bass.ds(i * 4 + j, 1)]), t + 1, At(G_M1 + j + 1, i, 4), tiles_taken)
                    conv_taps(c, *taps[2])
            op.leave(3, per, start=1)
            op.settle()
            dve.tensor_scalar(acc[:], acc[:], 1.0 / H, None, ALU.mult).then_inc(mean_sum_ready, 1)
            for j in range(4):
                u, t = At(U_M1 + 36 + 3 * j), At(T_M1 + 24 + 2 * j)
                step(u)
                step(u + 1)
                scale_tile(scaled[:], t)
                if j == 0:
                    dve.wait_ge(spread_done, 2)
                    op(dve.tensor_copy(tmp[:], ps[:, 7]))
                    op(dve.memset(acc[:], 0.0))
                    op.settle()
                step(u + 2)
                gated(merged[:, 12 + j], t + 1, At(G_M1 + 12 + j + 1), tiles_taken)
                for c in (2 * j, 2 * j + 1):
                    dve.tensor_tensor(a_conv[:, c, PAD:], a_conv[:, c, PAD:], tmp[:], ALU.subtract).then_inc(centred, 1)
                for c in (2 * j, 2 * j + 1):
                    dve.wait_ge(squares_ready, c + 1)
                    if c > 0:
                        dve.wait_ge(squares_added, c)
                    dve.tensor_tensor(acc[:], acc[:], sq[:, c % 2], ALU.add).then_inc(squares_added, 1)

            def conv_branch(u, t, m, sigmoids, within_gate=None):
                step(u)
                if within_gate:
                    within_gate()
                step(u + 1)
                scale_tile(scaled[:], t)
                step(u + 2)
                gated(tmp[:], t + 1, sigmoids, tiles_taken)
                dve.wait_ge(tiles_taken, (t + 2).value())
                dve.tensor_tensor(m, m, tmp[:], ALU.add).then_inc(merged_ready, 1)

            def layer_norm():
                token_factors(2)
                factors_on_all(2, 3, 7, acc)
                for c in range(HC):
                    if c >= 2:
                        dve.wait_ge(silu_ready, c - 1)
                    dve.scalar_tensor_tensor(out=(scaled, conv_acc)[c % 2][:], in0=a_conv[:, c, PAD:], scalar=param(C_LNG, At(c)),
                                             in1=acc[:], op0=ALU.mult, op1=ALU.mult).then_inc(ln_scaled, 1)
                    if c > 0:
                        dve.wait_ge(a_hi_ready, c)
                        low(a_lo[:, c - 1], tmp[:], a_hi[:, c - 1], a_ready)
                dve.wait_ge(a_hi_ready, HC)
                low(a_lo[:, HC - 1], tmp[:], a_hi[:, HC - 1], a_ready)

            conv_branch(At(U_M2), At(T_M2), merged[:, 0], At(G_M2 + 1), within_gate=layer_norm)
            for m in range(1, 4):
                conv_branch(At(U_M2 + 3 * m), At(T_M2 + 2 * m), merged[:, m], At(G_M2 + m + 1))
            with dve.Fori(1, DC // 4) as i:
                for j in range(4):
                    conv_branch(At(U_M2 + 3 * j, i, 12), At(T_M2 + 2 * j, i, 8), flat(merged[:, bass.ds(i * 4 + j, 1)]),
                                At(G_M2 + j + 1, i, 4))
            for c in range(DC):
                dve.wait_ge(merged_hi_ready, c + 1)
                low(xg_lo[:, c], merged[:, c], xg_hi[:, c], merged_split)

            dve.wait_ge(gain_o_in, 16)
            for n in range(NG):
                for v in range(DC // 2):
                    step(At(U_O + 8 * n + v))
                for b in range(BLK):
                    dve.wait_ge(squares_ready, Q_O + 4 * n + b + 1)
                    dve.tensor_tensor(og[:, n, b], ps[:, 4 * (n % 2) + b], gain_o[:, n], ALU.mult).then_inc(tiles_taken, 1)
            sum_groups(Q_O + DC)
            dve.wait_ge(x_back, 16 * NG)
            token_factors(3)

            def x2_group(n):
                for b in range(BLK):
                    if n == 0 and b == 0:
                        dve.wait_ge(tiles_taken, T_F)
                    add_rows(x2[:, n, b], og[:, n, b], b, x2[:, n, b], x2_ready)

            x2_group(0)
            for c in range(DC):
                if c % 4 == 0 and c < 12:
                    x2_group(c // 4 + 1)
                dve.wait_ge(turned_hi, DC + c + 1)
                scaled_low(xg_lo[:, c], ps[:, c % 4], param(C_FFNPRE, At(c)), xg_hi[:, c], turned_split)
                if c == 11:
                    step(At(U_F))
                    step(At(U_F + 1))
            token_factors(4)
            factors_on_all(3, 4, 3, r_bc)

            op(dve.memset(up_gate[:, 0:2], 0.0))
            op(dve.memset(up_val[:, 0:2], 0.0))

            def up(u, t, q, half, first=False):
                def last_taps(dst, src, c, j, tally):
                    dve.wait_ge(first_tap_ready, At(2 * (q.c + c) + j + 1, q.i, 2 * q.k).value())
                    op(dve.scalar_tensor_tensor(out=dst[:], in0=src[:, 1:1 + TOK], scalar=param(C_CFW + 2 * FC + j * FC, q + c),
                                                in1=dst[:], op0=ALU.mult, op1=ALU.add))
                    op.settle()
                    tally(dve.scalar_tensor_tensor(out=dst[:], in0=src[:, 2:2 + TOK], scalar=param(C_CFW + 4 * FC + j * FC, q + c),
                                                   in1=dst[:], op0=ALU.mult, op1=ALU.add))

                def product(c):
                    last_taps(val_c, up_val, c, 1, op)
                    op.settle()
                    dve.wait_ge(gelu_ready, (q + (c + 1)).value())
                    dve.tensor_tensor(ff_prod[:], gelu_g[:], val_c[:], ALU.mult).then_inc(ff_ready, 1)

                def product_low(c):
                    dve.wait_ge(g_hi_ready, (q + (c + 1)).value())
                    low(g_lo[:, half, c], ff_prod[:], g_hi[:, half, c], g_ready)

                def gate_taps(c):
                    last_taps(gate_c, up_gate, c, 0, lambda ins: ins.then_inc(gate_conv_ready, 1))

                for c in range(GRP):
                    take = lambda dst, w: scale_tile(dst[:, 2:], t + w, bank=(w + 4) % 8)
                    if first and c == 0:
                        step(u + 2)
                        step(u + 3)
                        take(up_gate, 0)
                        gate_taps(c)
                        take(up_val, 1)
                        continue
                    step(u + 4 * c)
                    if c > 0:
                        product(c - 1)
                    step(u + (4 * c + 1))
                    if c > 0:
                        product_low(c - 1)
                    take(up_gate, 2 * c)
                    step(u + (4 * c + 2))
                    gate_taps(c)
                    step(u + (4 * c + 3))
                    take(up_val, 2 * c + 1)
                product(GRP - 1)
                product_low(GRP - 1)

            def down(u, t, last=False):
                for n in range(NG):
                    for v in range(2):
                        step(u + (2 * n + v))
                    for b in range(BLK):
                        dve.tensor_tensor(f_acc[:, n, b], f_acc[:, n, b], ps[:, 4 * ((n + 1) % 2) + b], ALU.add).then_inc(tiles_taken, 1)
                    if last:
                        for b in range(BLK):
                            dve.wait_ge(squares_ready, Q_F + 4 * n + b + 1)
                            op(dve.tensor_tensor(f_acc[:, n, b], f_acc[:, n, b], gain_f[:, n], ALU.mult))

            up(At(F_UP(0)), At(FT_UP(0)), At(0), 0, first=True)
            dve.wait_ge(f_zero, 1)
            per = 2 * GRP * 3
            with dve.Fori(0, (NGRP - 1) // 2) as i:
                op.enter(i, per)
                for s in range(2):
                    up(At(F_UP(1 + s), i, 48), At(FT_UP(1 + s), i, 48), At(GRP * (1 + s), i, 2 * GRP), 1 - s)
                    down(At(F_DOWN(s), i, 48), At(FT_DOWN(s), i, 48))
            op.leave((NGRP - 1) // 2, per)
            for k in range(PLEC):
                dve.wait_ge(p_hi_ready, k + 1)
                low(p_lo[:, k], ps[:, k], p_hi[:, k], p_ready)
            dve.wait_ge(gain_f_in, 16)
            down(At(F_DOWN(NGRP - 1)), At(FT_DOWN(NGRP - 1)), last=True)
            sum_groups(Q_F + DC)
            op.settle()
            dve.wait_ge(x2_in, 16)
            token_factors(5)
            for n in range(NG):
                for b in range(BLK):
                    add_rows(x3[:, n, b], f_acc[:, n, b], b, x3[:, n, b], x3_ready)
                step(At(U_L + n))
            for c in range(DC):
                dve.wait_ge(turned_hi, 2 * DC + c + 1)
                low(x3_lo[:, c], ps[:, c % 4], x3_hi[:, c], turned_split)
                if c % 4 == 3 and c > 4:
                    step(At(U_G + c // 4 - 1))

            for n in range(NG):
                for v in range(3 if n == 0 else 0, DC // 2):
                    if U_G + 8 * n + v + SLOTS < U_END:
                        step(At(U_G + 8 * n + v))
                for b in range(BLK):
                    dve.wait_ge(sigmoid_ready, G_G + 4 * n + b + 1)
                    dve.tensor_tensor(e_buf[:, n, b], e_buf[:, n, b], (sig, scaled)[b % 2][:], ALU.mult).then_inc(tiles_taken, 1)
                if n == 0:
                    dve.wait_ge(gain_e_in, 16)
                for b in range(BLK):
                    dve.wait_ge(squares_ready, Q_E + 4 * n + b + 1)
                    op(dve.tensor_tensor(e_buf[:, n, b], e_buf[:, n, b], gain_e[:, n], ALU.mult))
            sum_groups(Q_E + DC)
            op.settle()
            token_factors(6)
            for n in range(NG):
                for b in range(BLK):
                    add_rows(e_buf[:, n, b], e_buf[:, n, b], b, x3[:, n, b], y_ready)


NAMES = ["x", "p", "mix_pre_g", "w_in", "conv_a_w", "conv_a_b", "ln_a_g", "ln_a_b", "w_a_out", "pool_w", "pool_scale",
         "w_b_out", "w_o", "mix_post_g", "ffn_pre_g", "w_up", "conv_f_w", "conv_f_b", "w_down", "ffn_post_g", "w_ple",
         "w_ple_gate", "ple_post_g"]


def kernel(**inputs):
    import concourse.bacc as bacc
    from concourse.bass_utils import run_bass_kernel_spmd

    nc = bacc.Bacc("TRN2", target_bir_lowering=False, num_devices=1)
    arrays, args = {}, []
    for name in NAMES:
        a = np.ascontiguousarray(inputs[name])
        arrays[f"in_{name}"] = a
        args.append(nc.dram_tensor(f"in_{name}", a.shape, mybir.dt.from_np(a.dtype), kind="ExternalInput").ap())
    out = nc.dram_tensor("out_0", (1, TOK, D), F32, kind="ExternalOutput").ap()
    build(nc, *args, out)
    r = run_bass_kernel_spmd(nc, [arrays], core_ids=[0])
    return r.results[0]["out_0"]
```

```python
from contextlib import ExitStack

import numpy as np

import concourse.bass as bass
from concourse import mybir

F32 = mybir.dt.float32
F32R = mybir.dt.float32r
ALU = mybir.AluOpType
ACT = mybir.ActivationFunctionType
AX = mybir.AxisListType

P = 128
TOK = 512
BLK = TOK // P
D = 2048
DC = D // P
W = 512
NG = D // W
H = D // 2
HC = H // P
FF = 5632
FC = FF // P
CONV_W = 31
PAD = CONV_W - 1
WINDOWS = (2, 4, 8, 16)
PGD = H // len(WINDOWS)
PPAD = 16
FTAPS = 3
PLE = 256
PLEC = PLE // P
EPS = 1e-6
GRP = 4
NGRP = FC // GRP

FIRST_SPLITS = (0, 1, 7, 8)
UNIT = 8 * P
RAW, SLOTS = 2, 4

U_A = 0
U_B = U_A + 4 * HC
U_M1 = U_B + 2 * HC + 2
U_M2 = U_M1 + 3 * DC
U_O = U_M2 + 3 * DC
U_F = U_O + 2 * DC
U_L = U_F + 4 * FC + 8 * NGRP
U_G = U_L + 4
U_END = U_G + 2 * DC
T_A = 0
T_B = T_A + 2 * HC
T_M1 = T_B + HC
T_M2 = T_M1 + 2 * DC
T_O = T_M2 + 2 * DC
T_F = T_O + DC
T_G = T_F + 2 * FC + DC * NGRP
F_UP = lambda j: U_F if j == 0 else U_F + 4 * GRP + 24 * (j - 1)
F_DOWN = lambda j: U_F + 4 * GRP + 24 * j + (4 * GRP if j < NGRP - 1 else 0)
FT_UP = lambda j: T_F if j == 0 else T_F + 2 * GRP + 24 * (j - 1)
FT_DOWN = lambda j: T_F + 2 * GRP + 24 * j + (2 * GRP if j < NGRP - 1 else 0)
EARLY = 7
MAP_BANKS = (1, 4, 5, 6, 2, 3, 7, 0)
G_A, G_M1, G_M2, G_G = 0, HC, HC + DC, HC + 2 * DC
Q_O, Q_F, Q_E = HC, HC + DC, HC + 2 * DC

C_MIXPRE, C_FFNPRE, C_CAB = 0, DC, 2 * DC
C_LNG = C_CAB + HC
C_LNB = C_LNG + HC
C_PSC = C_LNB + HC
C_CAW = C_PSC + HC
C_CFB = C_CAW + CONV_W * HC
C_CFW = C_CFB + 2 * FC
C_ALL = C_CFW + FTAPS * 2 * FC


class At:

    def __init__(self, c, i=None, k=0):
        self.c, self.i, self.k = c, i, k

    def __add__(self, n):
        return At(self.c + n, self.i, self.k)

    def value(self):
        return self.c if self.i is None or self.k == 0 else self.i * self.k + self.c

    def slot(self, n):
        assert self.k % n == 0
        return self.c % n

    def raw_count(self):
        assert self.k % RAW == 0
        return At(16 * (self.c // RAW + 1), self.i, 16 * self.k // RAW)


class Tally:

    def __init__(self, eng, sem):
        self.eng, self.sem, self.at = eng, sem, At(0)

    def __call__(self, ins):
        ins.then_inc(self.sem, 1)
        self.at = self.at + 1

    def settle(self, but=0):
        self.eng.wait_ge(self.sem, (self.at + -but).value())

    def enter(self, i, per, start=0):
        self.base = self.at.c - start * per
        self.at = At(self.base, i, per)

    def leave(self, n, per, start=0):
        assert self.at.c - self.base == per, f"the loop adds {self.at.c - self.base}, not {per}"
        self.at = At(self.base + n * per)


def build(nc, x, p, mix_pre_g, w_in, conv_a_w, conv_a_b, ln_a_g, ln_a_b, w_a_out, pool_w, pool_scale, w_b_out,
          w_o, mix_post_g, ffn_pre_g, w_up, conv_f_w, conv_f_b, w_down, ffn_post_g, w_ple, w_ple_gate,
          ple_post_g, out):
    x2_dram = nc.dram_tensor("x2_dram", (P, NG, BLK, W), F32, kind="Internal").ap()
    rows_of = lambda a: a.rearrange("a (b t) (n f) -> t n (a b) f", t=P, f=W)
    ctx = ExitStack()
    with ctx:
        sem = lambda name: ctx.enter_context(nc.semaphore(name))

        cursor = [16512]

        def region(nbytes):
            at = cursor[0]
            cursor[0] += (nbytes + 63) // 64 * 64
            return at

        def place(name, shape, dt, offset):
            return nc.alloc_sbuf_tensor_at(name, shape, dt, offset=offset)

        FULL = DC * TOK * 4
        r_raw, r_whi, r_wlo = region(RAW * UNIT * 4), region(SLOTS * UNIT * 4), region(SLOTS * UNIT * 4)
        r1, r2, r3, r4 = region(FULL), region(FULL), region(FULL), region(FULL)
        r5 = region(HC * (PAD + TOK) * 4)
        w_raw = place("w_raw", [P, RAW, UNIT], F32, r_raw)
        w_hi = place("w_hi", [P, SLOTS, UNIT], F32R, r_whi)
        w_lo = place("w_lo", [P, SLOTS, UNIT], F32R, r_wlo)
        xg_hi = place("xg_hi", [P, DC, TOK], F32R, r1)
        xg_lo = place("xg_lo", [P, DC, TOK], F32R, r2)
        x3 = place("x3", [P, NG, BLK, W], F32, r1)
        x3_hi = place("x3_hi", [P, DC, TOK], F32R, r2)
        pooled_hi = place("pooled_hi", [P, HC, TOK], F32R, r3)
        pooled_lo = place("pooled_lo", [P, HC, TOK], F32R, r3 + FULL // 2)
        merged = place("merged", [P, DC, TOK], F32, r3)
        x2 = place("x2", [P, NG, BLK, W], F32, r3)
        f_acc = place("f_acc", [P, NG, BLK, W], F32, r3)
        x3_lo = place("x3_lo", [P, DC, TOK], F32R, r3)
        x_nat = place("x_nat", [P, NG, BLK, W], F32, r4)
        r_pool = r4 + FULL - 3 * 4 * (PPAD + TOK) - 4 * TOK
        u_pool = place("u_pool", [P, PPAD + TOK], F32, r_pool)
        s_pool = place("s_pool", [P, 2, PPAD + TOK], F32, r_pool + 4 * (PPAD + TOK))
        pool_f = place("pool_f", [P, TOK], F32, r_pool + 12 * (PPAD + TOK))
        mixed_hi = place("mixed_hi", [P, HC, TOK], F32R, r4)
        mixed_lo = place("mixed_lo", [P, HC, TOK], F32R, r4 + FULL // 2)
        a_hi = place("a_hi", [P, HC, TOK], F32R, r4)
        a_lo = place("a_lo", [P, HC, TOK], F32R, r4 + FULL // 2)
        og = place("og", [P, NG, BLK, W], F32, r4)
        g_hi = place("g_hi", [P, 2, GRP, TOK], F32R, r4)
        g_lo = place("g_lo", [P, 2, GRP, TOK], F32R, r4 + FULL // 2)
        e_buf = place("e_buf", [P, NG, BLK, W], F32, r4)
        par_nat = place("par_nat", [P, 7, P], F32, r5)
        gain0_nat = place("gain0_nat", [DC, P], F32, r5 + 4096)
        squares_out = place("squares_out", [P, NG, W], F32, r5 + D * 4)
        a_conv = place("a_conv", [P, HC, PAD + TOK], F32, r5)
        gain_o = place("gain_o", [P, NG, W], F32, r5)
        up_gate = place("up_gate", [P, 2 + TOK], F32, r5)
        up_val = place("up_val", [P, 2 + TOK], F32, r5 + 2112)
        gate_c = place("gate_c", [P, TOK], F32, r5 + 4224)
        val_c = place("val_c", [P, TOK], F32, r5 + 6272)
        gelu_g = place("gelu_g", [P, TOK], F32, r5 + 8320)
        ff_prod = place("ff_prod", [P, TOK], F32, r5 + 10368)
        gain_f = place("gain_f", [P, NG, W], F32, r2 + FULL - 4 * D)
        p_nat = place("p_nat", [P, BLK, PLE], F32, r5)
        p_hi = place("p_hi", [P, PLEC, TOK], F32R, r5 + 4096)
        p_lo = place("p_lo", [P, PLEC, TOK], F32R, r5 + 8192)
        gain_e = place("gain_e", [P, NG, W], F32, r5)
        small = lambda name, shape: place(name, shape, F32, region(4 * int(np.prod(shape[1:]))))
        par = small("par", [P, C_ALL])
        ident = small("ident", [P, P])
        ones = small("ones", [P, P])
        diag = small("diag", [P, BLK, P])
        r_bc = small("r_bc", [P, TOK])
        sq = small("sq", [P, 2, TOK])
        acc = small("acc", [P, TOK])
        scaled = small("scaled", [P, TOK])
        sig = small("sig", [P, TOK])
        tmp = small("tmp", [P, TOK])
        conv_acc = small("conv_acc", [P, TOK])
        sums = small("sums", [P, BLK, NG])
        row_sum = small("row_sum", [P, BLK])
        std = small("std", [P, BLK])
        rstd = small("rstd", [P, BLK])
        eps = small("eps", [P, 1])
        unused = small("unused", [P, 1])
        inv_count = small("inv_count", [P, PPAD])
        assert cursor[0] <= nc.sbuf_usable_end, cursor[0]
        ps = ctx.enter_context(nc.psum_tensor("ps", [P, 8, TOK], F32))

        raw_in = [sem(f"raw_in{s}") for s in range(RAW)]
        slots_freed = sem("slots_freed")
        hi_ready, lo_ready, units_done = sem("hi_ready"), sem("lo_ready"), sem("units_done")
        blocks_done = sem("blocks_done")
        tiles_taken, dve_chain = sem("tiles_taken"), sem("dve_chain")
        x_in = [sem(f"x_in{n}") for n in range(NG)]
        par_in0, par_in1 = sem("par_in0"), sem("par_in1")
        consts_ready, ident_zero, table_loaded = sem("consts_ready"), sem("ident_zero"), sem("table_loaded")
        par_turned, par_ready = sem("par_turned"), sem("par_ready")
        turned, turned_hi, turned_split = sem("turned"), sem("turned_hi"), sem("turned_split")
        row_squares, row_sums_ready, x2_ready, x3_ready = (sem(n) for n in ("row_squares", "row_sums_ready", "x2_ready", "x3_ready"))
        mean_sum_ready, sums_done, std_ready = sem("mean_sum_ready"), sem("sums_done"), sem("std_ready")
        diag_ready, spread_done = sem("diag_ready"), sem("spread_done")
        pool_f_ready, pooled_hi_ready, pooled_ready = sem("pool_f_ready"), sem("pooled_hi_ready"), sem("pooled_ready")
        mixed_hi_ready, mixed_ready, sigmoid_ready = sem("mixed_hi_ready"), sem("mixed_ready"), sem("sigmoid_ready")
        centred, squares_ready, squares_added = sem("centred"), sem("squares_ready"), sem("squares_added")
        ln_scaled, silu_ready, a_hi_ready, a_ready = (sem(n) for n in ("ln_scaled", "silu_ready", "a_hi_ready", "a_ready"))
        merged_ready, merged_hi_ready, merged_split = (sem(n) for n in ("merged_ready", "merged_hi_ready", "merged_split"))
        first_tap_ready, gate_conv_ready, gelu_ready = (sem(n) for n in ("first_tap_ready", "gate_conv_ready", "gelu_ready"))
        ff_ready, g_hi_ready, g_ready = sem("ff_ready"), sem("g_hi_ready"), sem("g_ready")
        ple_taken, y_ready = sem("ple_taken"), sem("y_ready")
        x_back, x2_out, f_zero = (sem(n) for n in ("x_back", "x2_out", "f_zero"))
        x2_in = [sem(f"x2_in{n}") for n in range(NG)]
        gain_o_in, gain_f_in, gain_e_in = sem("gain_o_in"), sem("gain_f_in"), sem("gain_e_in")
        p_in, p_turned, p_hi_ready, p_ready = sem("p_in"), sem("p_turned"), sem("p_hi_ready"), sem("p_ready")
        out_done = sem("out_done")

        block = ctx.enter_context(nc.Block())

        @block.sync
        def _(sp):
            for_k = lambda w: w.rearrange("(k p) n -> p k n", p=P)
            win, wa, wb, wo = for_k(w_in), for_k(w_a_out), for_k(w_b_out), for_k(w_o)
            wup, wdn, wpg, wpl = for_k(w_up), for_k(w_down), for_k(w_ple_gate), for_k(w_ple)

            def load(u, src, width):
                if not (u.i is None and u.c < RAW):
                    sp.wait_ge(lo_ready, (u + (1 - RAW)).value())
                    sp.sem_inc(slots_freed, 1)
                s = u.slot(RAW)
                sp.dma_start(w_raw[:, s].rearrange("p (k n) -> p k n", n=width), src).then_inc(raw_in[s], 16)

            def half_column(u, w, col, h):
                load(u, w[:, 8 * h:8 * h + 8, bass.ds(col, P)], P)

            def column(u, w, col):
                for h in range(2):
                    half_column(u + h, w, col, h)

            def pair(u, w, cols):
                for h in range(2):
                    for j in range(2):
                        half_column(u + (2 * h + j), w, cols[j], h)

            def rows(u, w, k, n):
                load(u, w[:, bass.ds(k, 2), bass.ds(n * W, W)], W)

            xr = rows_of(x)
            sp.dma_start(x_nat[:, 0], xr[:, 0]).then_inc(x_in[0], 16)
            for j in range(2):
                half_column(At(U_A + j), win, (H, 0)[j], 0)
            for n in range(1, NG):
                sp.dma_start(x_nat[:, n], xr[:, n]).then_inc(x_in[n], 16)
            for j in range(2):
                half_column(At(U_A + 2 + j), win, (H, 0)[j], 1)
            with sp.Fori(1, HC) as c:
                column(At(U_A, c, 4), win, c * P + H)
                column(At(U_A + 2, c, 4), win, c * P)
            with sp.Fori(0, HC) as c:
                column(At(U_B, c, 2), win, c * P + 2 * H)
            column(At(U_M1 - 2), win, 3 * H + D)
            pw = pool_w.rearrange("g (k p) d -> p (g k) d", p=P)
            for n in range(2):
                load(At(U_M1 + n), pw[:, 4 * n:4 * n + 4, :], PGD)
            half_column(At(U_M1 + 2), wb, 0, 0)
            column(At(U_M1 + 3), win, 3 * H + D + P)
            half_column(At(U_M1 + 5), wb, P, 0)
            for first, start, w, gates in ((U_M1, 1, wb, 3 * H + D), (U_M2, 0, wa, 3 * H)):
                with sp.Fori(start, DC // 2) as m2:
                    for j in range(2):
                        column(At(first + 3 * j, m2, 6), win, m2 * (2 * P) + (gates + j * P))
                        half_column(At(first + 3 * j + 2, m2, 6), w, m2 * (2 * P) + j * P, 0)
            with sp.Fori(0, NG) as n:
                for v in range(DC // 2):
                    rows(At(U_O + v, n, 8), wo, 2 * v, n)
            pair(At(F_UP(0)), wup, (0, FF))
            with sp.Fori(1, GRP) as c:
                column(At(F_UP(0), c, 4), wup, c * P)
                column(At(F_UP(0) + 2, c, 4), wup, c * P + FF)
            with sp.Fori(0, NGRP - 1) as j:
                for c in range(GRP):
                    column(At(F_UP(1) + 4 * c, j, 24), wup, j * (GRP * P) + (GRP + c) * P)
                    column(At(F_UP(1) + 4 * c + 2, j, 24), wup, j * (GRP * P) + ((GRP + c) * P + FF))
                for n in range(NG):
                    for v in range(GRP // 2):
                        rows(At(F_DOWN(0) + 2 * n + v, j, 24), wdn, j * GRP + 2 * v, n)
            with sp.Fori(0, NG) as n:
                for v in range(GRP // 2):
                    rows(At(F_DOWN(NGRP - 1) + v, n, 2), wdn, (NGRP - 1) * GRP + 2 * v, n)
            for n in range(NG):
                rows(At(U_L + n), wpl, 0, n)
            with sp.Fori(0, NG) as n:
                for v in range(DC // 2):
                    rows(At(U_G + v, n, 8), wpg, 2 * v, n)
            for b in range(BLK):
                sp.wait_ge(y_ready, NG * (b + 1))
                sp.dma_start(rows_of(out)[:, :, b], e_buf[:, :, b]).then_inc(out_done, 16)
            sp.wait_ge(out_done, 16 * BLK)

        @block.gpsimd
        def _(pool):
            on_all = lambda g: g.partition_broadcast(P).rearrange("p (n f) -> p n f", f=W)
            nc.gpsimd.memset(ident[:], 0.0).then_inc(ident_zero, 1)
            pool.wait_ge(ident_zero, 1)
            nc.gpsimd.affine_select(out=ident[:], in_=ident[:], compare_op=ALU.not_equal, fill=1.0, base=0,
                                    pattern=[[-1, P]], channel_multiplier=1).then_inc(consts_ready, 1)
            nc.gpsimd.memset(ones[:], 1.0).then_inc(consts_ready, 1)
            nc.gpsimd.memset(eps[:], EPS).then_inc(consts_ready, 1)
            for t in range(PPAD):
                nc.gpsimd.memset(inv_count[:, t:t + 1], 1.0 / (t + 1)).then_inc(consts_ready, 1)
            pool.wait_ge(a_ready, HC)
            pool.dma_start(gain_o[:], on_all(mix_post_g)).then_inc(gain_o_in, 16)
            pool.wait_ge(x2_ready, NG * BLK)
            pool.dma_start(x2_dram, x2[:]).then_inc(x2_out, 16)
            pool.wait_ge(x2_out, 16)
            pool.wait_ge(row_squares, 2 * BLK)
            pool.wait_ge(turned, 2 * DC)
            nc.gpsimd.memset(f_acc[:], 0.0).then_inc(f_zero, 1)
            pool.wait_ge(units_done, F_UP(NGRP - 1) + 4 * GRP)
            pool.dma_start(gain_f[:], on_all(ffn_post_g)).then_inc(gain_f_in, 16)
            pool.wait_ge(g_ready, FC)
            pool.dma_start(p_nat[:], p.rearrange("z a (b t) d -> t (z a b) d", t=P)).then_inc(p_in, 16)
            for n in range(NG):
                pool.wait_ge(units_done, F_DOWN(NGRP - 2) + 2 * n + 1)
                pool.dma_start(x3[:, n], x2_dram[:, n]).then_inc(x2_in[n], 16)
            pool.wait_ge(units_done, U_G)
            pool.dma_start(gain_e[:], on_all(ple_post_g)).then_inc(gain_e_in, 16)

        @block.tensor
        def _(pe):
            pe.wait_ge(consts_ready, 2)

            def bank_free(t, banks):
                if not (t.i is None and t.c < banks):
                    pe.wait_ge(tiles_taken, (t + (1 - banks)).value())

            def products(o, s, cols, hi, lo, start, stop):
                pe.matmul(o, w_hi[:, s, cols], hi, start=start, stop=False)
                pe.matmul(o, w_hi[:, s, cols], lo, start=False, stop=False)
                return pe.matmul(o, w_lo[:, s, cols], hi, start=False, stop=stop)

            def chunk_products(o, u, k, hi, lo, chunks):
                last = products(o, u.slot(SLOTS), slice(k % 8 * P, (k % 8 + 1) * P), hi[:, k], lo[:, k], k == 0, k == chunks - 1)
                if k % 8 == 7:
                    last.then_inc(units_done, 1)

            def tile(u, t, hi, lo, chunks=DC, arrives=None, bank=None, banks=4, between=None):
                bank_free(t, banks)
                for k in range(chunks):
                    if k % 8 == 0:
                        if k and between:
                            between()
                        pe.wait_ge(lo_ready, (u + (k // 8 + 1)).value())
                    if arrives is not None:
                        pe.wait_ge(arrives, k + 1)
                    chunk_products(ps[:, t.slot(4) if bank is None else bank], u + k // 8, k, hi, lo, chunks)

            def turn(src, base, c, bank0):
                if c >= BLK:
                    pe.wait_ge(turned_split, base + c - 3)
                n, q = c // 4, c % 4
                for b in range(BLK):
                    mm = pe.transpose(ps[:, bank0 + q, b * P:(b + 1) * P], src[:, n, b, q * P:(q + 1) * P], ident[:])
                mm.then_inc(turned, 1)

            def first_pair(u, src, base, arrived, tile_bank, turn_bank):
                def turns(n):
                    if n < NG:
                        arrived(n)
                        for c in range(4 * n, 4 * n + 4):
                            turn(src, base, c, turn_bank)
                turns(0)
                for k in range(DC):
                    if k % 4 == 2:
                        turns(k // 4 + 1)
                    pe.wait_ge(turned_split, base + k + 1)
                    for j in range(2):
                        if k % 8 == 0:
                            pe.wait_ge(lo_ready, u + 2 * (k // 8) + j + 1)
                        chunk_products(ps[:, tile_bank + j], At(u + 2 * (k // 8) + j), k, xg_hi, xg_lo, DC)

            def rows(u, t, bank0, x_hi, x_lo, chunks, wait=None, ahead=None, by_block=0):
                nv = chunks // 2
                order = [(v, b) for v in range(nv - by_block) for b in range(BLK)]
                order += [(v, b) for b in range(BLK) for v in range(nv - by_block, nv)]
                for v, b in order:
                    if b == 0:
                        if ahead is not None:
                            ahead(v)
                        pe.wait_ge(lo_ready, (u + (v + 1)).value())
                        if wait is not None:
                            pe.wait_ge(wait[0], wait[1] + 2 * v + 2)
                    if v == 0 and t is not None:
                        bank_free(t + b, 8)
                    for kk in range(2):
                        k, o = 2 * v + kk, ps[:, bank0 + b]
                        cols, tok, s = slice(kk * W, (kk + 1) * W), slice(b * P, (b + 1) * P), (u + v).slot(SLOTS)
                        pe.matmul(o, x_hi[:, k, tok], w_hi[:, s, cols], start=k == 0, stop=False)
                        pe.matmul(o, x_lo[:, k, tok], w_hi[:, s, cols], start=False, stop=False)
                        last = pe.matmul(o, x_hi[:, k, tok], w_lo[:, s, cols], start=False, stop=k == chunks - 1)
                    if b == BLK - 1:
                        last.then_inc(units_done, 1)
                    elif by_block and v == nv - 1:
                        last.then_inc(blocks_done, 1)

            def spread(n, bank):
                pe.wait_ge(diag_ready, n)
                for b in range(BLK):
                    mm = pe.matmul(ps[:, bank, b * P:(b + 1) * P], ones[:], diag[:, b], start=True, stop=True)
                mm.then_inc(spread_done, 1)

            pe.wait_ge(par_in0, 16)
            pe.transpose(ps[:, 2, 0:DC], gain0_nat[:], ident[0:DC, 0:DC]).then_inc(par_turned, 1)
            first_pair(U_A, x_nat, 0, lambda n: pe.wait_ge(x_in[n], 16), 0, 4)
            pe.wait_ge(par_in1, 16 * 12)
            n = CONV_W * HC // 2
            pe.transpose(ps[:, 5, 0:C_CAW], par_nat[0:C_CAW, 0], ident[0:C_CAW, 0:C_CAW])
            for j in range(2):
                pe.transpose(ps[:, 5, C_CAW + j * n:C_CAW + (j + 1) * n], par_nat[0:n, 1 + j], ident[0:n, 0:n])
            n = 2 * FC
            for j in range(1 + FTAPS):
                mm = pe.transpose(ps[:, 6, j * n:(j + 1) * n], par_nat[0:n, 3 + j], ident[0:n, 0:n])
            mm.then_inc(par_turned, 1)
            pe.wait_ge(par_ready, 1)
            tile(At(U_A + 4), At(T_A + 2), xg_hi, xg_lo, between=lambda: spread(1, 7))
            tile(At(U_A + 6), At(T_A + 3), xg_hi, xg_lo)
            with pe.Fori(1, HC // 2) as i:
                for j in range(4):
                    tile(At(U_A + 2 * j, i, 8), At(T_A + j, i, 4), xg_hi, xg_lo)
            with pe.Fori(0, 2) as i:
                for j in range(4):
                    tile(At(U_B + 2 * j, i, 8), At(T_B + j, i, 4), xg_hi, xg_lo)
            tile(At(U_M1 - 2), At(T_M1), xg_hi, xg_lo)
            for c in range(HC):
                u, g, mo = At(U_M1 + c // 4), c // 2, c % 2
                if c % 4 == 0:
                    pe.wait_ge(lo_ready, (u + 1).value())
                if c == 0:
                    pe.wait_ge(tiles_taken, T_M1)
                if c == 7:
                    pe.wait_ge(tiles_taken, T_M1 + 1)
                pe.wait_ge(pooled_ready, 2 * g + 2)
                for k in range(2):
                    at = (2 * (g % 2) + k) * PGD + mo * P
                    last = products(ps[:, MAP_BANKS[c]], u.slot(SLOTS), slice(at, at + P),
                                    pooled_hi[:, 2 * g + k], pooled_lo[:, 2 * g + k], k == 0, k == 1)
                if c % 4 == 3:
                    last.then_inc(units_done, 1)

            def branch(u, t, hi, lo, arrives=None, ahead_of_branch=None, within_gate=None, gate=True):
                if gate:
                    tile(u, t, xg_hi, xg_lo, between=within_gate)
                if ahead_of_branch:
                    ahead_of_branch()
                tile(u + 2, t + 1, hi, lo, chunks=HC, arrives=arrives)

            for m in range(4):
                branch(At(U_M1 + 3 * m), At(T_M1 + 2 * m), mixed_hi, mixed_lo, gate=m > 0, arrives=mixed_ready if m == 0 else None)
            with pe.Fori(1, 3) as i:
                for j in range(4):
                    branch(At(U_M1 + 3 * j, i, 12), At(T_M1 + 2 * j, i, 8), mixed_hi, mixed_lo)

            def mean():
                pe.wait_ge(mean_sum_ready, 1)
                pe.matmul(ps[:, 7], ones[:], acc[:], start=True, stop=True).then_inc(spread_done, 1)

            def variance():
                pe.wait_ge(squares_added, HC)
                for b in range(BLK):
                    mm = pe.matmul(ps[:, 4, b:b + 1], acc[:, b * P:(b + 1) * P], ones[:, 0:1], start=True, stop=True)
                mm.then_inc(sums_done, 1)

            for m in range(12, DC):
                branch(At(U_M1 + 3 * m), At(T_M1 + 2 * m), mixed_hi, mixed_lo, within_gate=(lambda: spread(2, 7)) if m == DC - 1 else None,
                       ahead_of_branch={12: mean, 14: variance}.get(m))

            for m in range(4):
                branch(At(U_M2 + 3 * m), At(T_M2 + 2 * m), a_hi, a_lo, arrives=a_ready if m == 0 else None)
            with pe.Fori(1, DC // 4) as i:
                for j in range(4):
                    branch(At(U_M2 + 3 * j, i, 12), At(T_M2 + 2 * j, i, 8), a_hi, a_lo)
            for n in range(NG):
                rows(At(U_O + 8 * n), At(T_O + 4 * n), 4 * ((n + 1) % 2), xg_hi, xg_lo, DC,
                     wait=(merged_split, 0) if n == 0 else None, by_block=2 if n == NG - 1 else 0)

            first_pair(U_F, x2, DC, lambda n: pe.wait_ge(x2_ready, BLK * (n + 1)), 0, 4)

            def up(u, t, first=False):
                for w in range(2 if first else 0, 2 * GRP):
                    if first and w == 2 * GRP - 1:
                        pe.wait_ge(tiles_taken, T_F + 1)
                    tile(u + 2 * w, t + w, xg_hi, xg_lo, bank=w, banks=8,
                         between=(lambda: spread(3, 7)) if first and w == 2 else None)

            def down(u, t, half):
                for n in range(NG):
                    rows(u + 2 * n, t + 4 * n, 4 * (n % 2), g_hi[:, half], g_lo[:, half], GRP)

            up(At(F_UP(0)), At(FT_UP(0)), first=True)
            with pe.Fori(0, (NGRP - 1) // 2) as i:
                for s in range(2):
                    up(At(F_UP(1 + s), i, 48), At(FT_UP(1 + s), i, 48))
                    pe.wait_ge(g_ready, At(GRP * (1 + s), i, 2 * GRP).value())
                    down(At(F_DOWN(s), i, 48), At(FT_DOWN(s), i, 48), s)
            pe.wait_ge(g_ready, FC)

            def turn_p(v):
                if v == 1:
                    pe.wait_ge(p_in, 16)
                    pe.wait_ge(tiles_taken, FT_DOWN(NGRP - 1))
                    for k in range(PLEC):
                        for b in range(BLK):
                            mm = pe.transpose(ps[:, 6 + k, b * P:(b + 1) * P], p_nat[:, b, k * P:(k + 1) * P], ident[:])
                    mm.then_inc(p_turned, 1)

            for n in range(NG):
                if n == 1:
                    pe.wait_ge(p_ready, PLEC)
                rows(At(F_DOWN(NGRP - 1) + 2 * n), At(FT_DOWN(NGRP - 1) + 4 * n), 4 * (n % 2), g_hi[:, 0], g_lo[:, 0], GRP,
                     ahead=turn_p if n == 0 else None, by_block=2 if n == NG - 1 else 0)
            for n in range(NG):
                if n < 2:
                    pe.wait_ge(tiles_taken, T_G - 4 + 4 * n)
                else:
                    pe.wait_ge(ple_taken, 4 * (n - 1))
                rows(At(U_L + n), None, 4 * (n % 2), p_hi, p_lo, PLEC, by_block=1)

            def turns(v):
                n = {0: 0, 1: 1, 3: 2, 5: 3}.get(v)
                if n is not None:
                    pe.wait_ge(x3_ready, BLK * (n + 1))
                    for c in range(4 * n, 4 * n + 4):
                        if c < 4:
                            pe.wait_ge(ple_taken, 4 * (NG - 1) + c + 1)
                        turn(x3, 2 * DC, c, 4)

            for n in range(NG):
                if n == 0:
                    pe.wait_ge(ple_taken, 4 * (NG - 1))
                if n == 1:
                    pe.wait_ge(turned_split, 3 * DC)
                rows(At(U_G + 8 * n), At(T_G + 4 * n) if n > 1 else None, 4 * (n % 2), x3_hi, x3_lo, DC,
                     wait=(turned_split, 2 * DC) if n == 0 else None, ahead=turns if n == 0 else None,
                     by_block=SLOTS if n == NG - 1 else 0)

        @block.scalar
        def _(act):
            f = act.activation

            def split(u):
                act.wait_ge(raw_in[u.slot(RAW)], u.raw_count().value())
                f(w_hi[:, u.slot(SLOTS)], w_raw[:, u.slot(RAW)], ACT.Copy).then_inc(hi_ready, 1)

            def step(u, ahead=True):
                act.wait_ge(units_done, (u + 1).value())
                if ahead:
                    split(u + SLOTS)

            def standard_deviation(total, src, blocks=slice(0, BLK)):
                f(std[:, blocks], src, ACT.Sqrt, bias=eps[:], scale=1.0 / total).then_inc(std_ready, 1)

            def row_squares_of(src, done):
                for b in range(BLK):
                    if done + b > 0:
                        act.wait_ge(row_squares, done + b)
                    f(squares_out[:], src[:, :, b], ACT.Square, accum_out=row_sum[:, b:b + 1]).then_inc(row_squares, 1)
                act.wait_ge(row_squares, done + BLK)

            def turned_high(base, c, bank0, dst, scale):
                act.wait_ge(turned, base + c + 1)
                f(dst[:, c], ps[:, bank0 + c % 4], ACT.Identity, scale=scale).then_inc(turned_hi, 1)

            def block_done(b, before, end):
                if b < BLK - 1:
                    act.wait_ge(blocks_done, before + b + 1)
                else:
                    act.wait_ge(units_done, end)

            def load_table(function):
                f(unused[:], eps[:], function).then_inc(table_loaded, 1)

            def tile_squares(src, b, n, k):
                act.wait_ge(squares_ready, k)
                f(sq[:, 0], src, ACT.Square, accum_out=sums[:, b, n:n + 1]).then_inc(squares_ready, 1)

            def param(base, q):
                return par[:, q.c + base:q.c + base + 1] if q.i is None else par[:, bass.ds(q.i * q.k + (q.c + base), 1)]

            as_rows = lambda v: v.rearrange("(c p) -> c p", p=P)
            act.dma_start(gain0_nat[:], as_rows(mix_pre_g)).then_inc(par_in0, 16)
            act.wait_ge(consts_ready, 3)
            load_table(ACT.Identity)
            taps = conv_a_w.rearrange("k (c p) -> (k c) p", p=P)
            n = CONV_W * HC // 2
            params = [(par_nat[col:col + v.shape[0] // P, 0], as_rows(v)) for col, v in
                      ((C_FFNPRE, ffn_pre_g), (C_CAB, conv_a_b), (C_LNG, ln_a_g), (C_LNB, ln_a_b), (C_PSC, pool_scale), (0, mix_pre_g))]
            params += [(par_nat[0:n, 1 + j], taps[j * n:(j + 1) * n]) for j in range(2)]
            params += [(par_nat[0:2 * FC, 3], as_rows(conv_f_b))]
            params += [(par_nat[0:2 * FC, 4 + k], as_rows(conv_f_w[k])) for k in range(FTAPS)]
            act.wait_ge(par_ready, 1)
            for c in range(DC):
                turned_high(0, c, 4, xg_hi, par[:, C_MIXPRE + c:C_MIXPRE + c + 1])
                if c in FIRST_SPLITS:
                    split(At(FIRST_SPLITS.index(c)))
                if c in (3, 7):
                    for to, src in params[0:6] if c == 3 else params[6:]:
                        act.dma_start(to, src).then_inc(par_in1, 16)
            for k in range(2):
                step(At(U_A + k))
            row_squares_of(x_nat, 0)
            standard_deviation(D, row_sum[:])

            def sigmoid(t):
                act.wait_ge(tiles_taken, (t + 1).value())
                f(sig[:], scaled[:], ACT.Sigmoid).then_inc(sigmoid_ready, 1)

            for k in range(2, 4):
                step(At(U_A + k))
            sigmoid(At(T_A))

            def glu(u, t):
                step(u)
                step(u + 1)
                sigmoid(t)
                step(u + 2)
                step(u + 3)

            glu(At(U_A + 4), At(T_A + 2))
            with act.Fori(1, HC // 2) as i:
                for j in range(2):
                    glu(At(U_A + 4 * j, i, 8), At(T_A + 2 * j, i, 4))
            for c in range(HC):
                step(At(U_B + 2 * c))
                step(At(U_B + 2 * c + 1))
                act.wait_ge(pool_f_ready, c + 1)
                f(pooled_hi[:, c], pool_f[:], ACT.Copy).then_inc(pooled_hi_ready, 1)

            def branch(u, t, within_gate=None, ahead_of_branch=None):
                step(u)
                if within_gate:
                    within_gate()
                step(u + 1)
                sigmoid(t)
                if ahead_of_branch:
                    ahead_of_branch()
                step(u + 2)

            step(At(U_M1 - 2))
            step(At(U_M1 - 1))
            sigmoid(At(T_M1))
            for n in range(2):
                act.wait_ge(units_done, U_M1 + n + 1)
                for c in range(4 * n, 4 * n + 4):
                    f(mixed_hi[:, c], ps[:, MAP_BANKS[c]], ACT.Identity,
                      scale=par[:, C_PSC + c:C_PSC + c + 1]).then_inc(mixed_hi_ready, 1)
                step(At(U_M1 + n))
            step(At(U_M1 + 2))
            for m in range(1, 4):
                branch(At(U_M1 + 3 * m), At(T_M1 + 2 * m))
            with act.Fori(1, 3) as i:
                for j in range(4):
                    branch(At(U_M1 + 3 * j, i, 12), At(T_M1 + 2 * j, i, 8))

            def centred_squares(c):
                act.wait_ge(centred, c + 1)
                if c >= 2:
                    act.wait_ge(squares_added, c - 1)
                f(sq[:, c % 2], a_conv[:, c, PAD:], ACT.Square).then_inc(squares_ready, 1)

            def layer_norm_factors():
                act.wait_ge(sums_done, 1)
                standard_deviation(H, ps[:, 4, 0:BLK])

            def swish(c):
                act.wait_ge(ln_scaled, c + 1)
                f(a_conv[:, c, PAD:], a_conv[:, c, PAD:], ACT.Silu, bias=par[:, C_LNB + c:C_LNB + c + 1]).then_inc(silu_ready, 1)

            for j in range(4):
                branch(At(U_M1 + 36 + 3 * j), At(T_M1 + 24 + 2 * j),
                       within_gate=(lambda: [swish(c) for c in range(4)]) if j == 3 else None)
                for c in range(4 * (j % 2), 4 * (j % 2) + 4):
                    if j < 2:
                        centred_squares(c)
                    elif j == 3:
                        swish(c)
                if j == 2:
                    layer_norm_factors()

            def conv_branch_high():
                for c in range(HC):
                    act.wait_ge(silu_ready, c + 1)
                    f(a_hi[:, c], a_conv[:, c, PAD:], ACT.Copy).then_inc(a_hi_ready, 1)

            def merged_high(chunks):
                for c in chunks:
                    act.wait_ge(merged_ready, c + 1)
                    f(xg_hi[:, c], merged[:, c], ACT.Copy).then_inc(merged_hi_ready, 1)

            branch(At(U_M2), At(T_M2), within_gate=conv_branch_high)
            for m in range(1, 4):
                branch(At(U_M2 + 3 * m), At(T_M2 + 2 * m))
            with act.Fori(1, DC // 4 - 1) as i:
                for j in range(4):
                    branch(At(U_M2 + 3 * j, i, 12), At(T_M2 + 2 * j, i, 8))
            for m in range(DC - 4, DC):
                branch(At(U_M2 + 3 * m), At(T_M2 + 2 * m),
                       ahead_of_branch=(lambda: merged_high(range(EARLY))) if m == DC - 1 else None)
            merged_high(range(EARLY, DC))
            act.wait_ge(merged_split, DC)
            for n in range(NG):
                act.dma_start(x2[:, n], rows_of(x)[:, n]).then_inc(x_back, 16)

            for n in range(NG):
                by_block = 2 if n == NG - 1 else 0
                for v in range(DC // 2 - by_block):
                    step(At(U_O + 8 * n + v))
                if n == 0:
                    load_table(ACT.Sqrt)
                for b in range(BLK):
                    if by_block:
                        block_done(b, 0, U_O + 8 * NG)
                    tile_squares(ps[:, 4 * ((n + 1) % 2) + b], b, n, Q_O + 4 * n + b)
                    if by_block and b >= BLK - 2:
                        act.wait_ge(row_sums_ready, b - 1)
                        blocks = slice(0, b + 1) if b == BLK - 2 else slice(b, BLK)
                        standard_deviation(D, row_sum[:, blocks], blocks)
            for k in (2, 1):
                step(At(U_F - k))
            for c in range(DC):
                turned_high(DC, c, 4, xg_hi, par[:, C_FFNPRE + c:C_FFNPRE + c + 1])
                if c == 11:
                    step(At(U_F))
                    step(At(U_F + 1))
            row_squares_of(x2, BLK)
            standard_deviation(D, row_sum[:])

            def up(u, t, q, half, first=False):
                def high(c):
                    act.wait_ge(ff_ready, (q + (c + 1)).value())
                    f(g_hi[:, half, c], ff_prod[:], ACT.Copy).then_inc(g_hi_ready, 1)

                def first_tap(dst, src, c, j):
                    act.wait_ge(tiles_taken, (t + (2 * c + j + 1)).value())
                    f(dst[:], src[:, 0:TOK], ACT.Identity, scale=param(C_CFW + j * FC, q + c),
                      bias=param(C_CFB + j * FC, q + c)).then_inc(first_tap_ready, 1)

                def gelu(c):
                    act.wait_ge(gate_conv_ready, (q + (c + 1)).value())
                    f(gelu_g[:], gate_c[:], ACT.Gelu_apprx_tanh).then_inc(gelu_ready, 1)

                for c in range(GRP):
                    if first and c == 0:
                        step(u + 2)
                        step(u + 3)
                        first_tap(gate_c, up_gate, c, 0)
                        gelu(c)
                    else:
                        step(u + 4 * c)
                        if c > 0:
                            high(c - 1)
                        step(u + (4 * c + 1))
                        first_tap(gate_c, up_gate, c, 0)
                        step(u + (4 * c + 2))
                        gelu(c)
                        step(u + (4 * c + 3))
                    first_tap(val_c, up_val, c, 1)
                high(GRP - 1)

            up(At(F_UP(0)), At(FT_UP(0)), At(0), 0, first=True)
            with act.Fori(0, (NGRP - 1) // 2) as i:
                for s in range(2):
                    up(At(F_UP(1 + s), i, 48), At(FT_UP(1 + s), i, 48), At(GRP * (1 + s), i, 2 * GRP), 1 - s)
                    for v in range(2 * NG):
                        step(At(F_DOWN(s) + v, i, 48))
            for n in range(NG):
                by_block = n == NG - 1
                for v in range(0 if by_block else 2):
                    step(At(F_DOWN(NGRP - 1) + 2 * n + v))
                    if n == 0 and v == 0:
                        act.wait_ge(p_turned, 1)
                        for k in range(PLEC):
                            f(p_hi[:, k], ps[:, 6 + k], ACT.Copy).then_inc(p_hi_ready, 1)
                for b in range(BLK):
                    act.wait_ge(tiles_taken, FT_DOWN(NGRP - 1) + 4 * n + b + 1)
                    tile_squares(f_acc[:, n, b], b, n, Q_F + 4 * n + b)
            act.wait_ge(row_sums_ready, 3)
            standard_deviation(D, row_sum[:])
            for k in (2, 1):
                step(At(U_L - k))
            for n in range(NG):
                if n < NG - 1:
                    for b in range(BLK):
                        block_done(b, 6 + 3 * n, U_L + n + 1)
                        f(e_buf[:, n, b], ps[:, 4 * (n % 2) + b], ACT.Copy).then_inc(ple_taken, 1)
                    step(At(U_L + n))
            for b in range(BLK):
                block_done(b, 6 + 3 * (NG - 1), U_L + NG)
                f(e_buf[:, NG - 1, b], ps[:, 4 * ((NG - 1) % 2) + b], ACT.Copy).then_inc(ple_taken, 1)
            for c in range(DC):
                turned_high(2 * DC, c, 4, x3_hi, 1.0)
                if c == 1:
                    step(At(U_L + NG - 1))
                if c % 4 == 3 and c > 4:
                    step(At(U_G + c // 4 - 1))
            for n in range(NG - 1):
                for v in range(3 if n == 0 else 0, DC // 2):
                    u = U_G + 8 * n + v
                    step(At(u), ahead=u + SLOTS < U_END)
                for b in range(BLK):
                    if 4 * n + b >= 2:
                        act.wait_ge(tiles_taken, T_G + 4 * n + b - 1)
                    f((sig, scaled)[b % 2][:], ps[:, 4 * (n % 2) + b], ACT.Sigmoid).then_inc(sigmoid_ready, 1)
                for b in range(BLK):
                    act.wait_ge(tiles_taken, T_G + 4 * n + b + 1)
                    tile_squares(e_buf[:, n, b], b, n, Q_E + 4 * n + b)
            n = NG - 1
            for v in range(DC // 2 - SLOTS):
                step(At(U_G + 8 * n + v))
            for b in range(BLK):
                block_done(b, 6 + 3 * NG, U_END)
                act.wait_ge(tiles_taken, T_G + 4 * n + b - 1)
                f((sig, scaled)[b % 2][:], ps[:, 4 * (n % 2) + b], ACT.Sigmoid).then_inc(sigmoid_ready, 1)
                act.wait_ge(tiles_taken, T_G + 4 * n + b + 1)
                tile_squares(e_buf[:, n, b], b, n, Q_E + 4 * n + b)
                if b == 1:
                    act.wait_ge(row_sums_ready, 4)
                    standard_deviation(D, row_sum[:, 0:2], slice(0, 2))
                if b == 2:
                    act.wait_ge(row_sums_ready, 5)
                    standard_deviation(D, row_sum[:, 2:3], slice(2, 3))
            act.wait_ge(row_sums_ready, 6)
            standard_deviation(D, row_sum[:, 3:4], slice(3, 4))

        @block.vector
        def _(dve):
            op = Tally(dve, dve_chain)
            as_f32 = lambda ap: ap.bitcast(F32)
            flat = lambda ap: ap.rearrange("p a t -> p (a t)")

            def step(u):
                split(u + SLOTS)

            def split(u):
                dve.wait_ge(hi_ready, (u + 1).value())
                s = u.slot(SLOTS)
                dve.tensor_tensor(w_lo[:, s], w_raw[:, u.slot(RAW)], as_f32(w_hi[:, s]), ALU.subtract).then_inc(lo_ready, 1)

            def scale_tile(dst, t, bank=None):
                dve.tensor_tensor(dst, ps[:, t.slot(4) if bank is None else bank], r_bc[:], ALU.mult).then_inc(tiles_taken, 1)

            def token_factors(n, blocks=slice(0, BLK)):
                dve.wait_ge(std_ready, n)
                op(dve.reciprocal(rstd[:, blocks], std[:, blocks]))
                op.settle()

            def diagonals():
                for b in range(BLK):
                    ins = dve.tensor_scalar(diag[:, b], ident[:], rstd[:, b:b + 1], None, ALU.mult)
                ins.then_inc(diag_ready, 1)

            def factors_spread(k, bank, dst):
                dve.wait_ge(spread_done, k)
                op(dve.tensor_copy(dst[:], ps[:, bank]))
                op.settle()

            def low(dst, src, hi, done):
                dve.tensor_tensor(dst, src, as_f32(hi), ALU.subtract).then_inc(done, 1)

            def scaled_low(dst, src, scale, hi, done):
                dve.scalar_tensor_tensor(out=dst, in0=src, scalar=scale, in1=as_f32(hi), op0=ALU.mult, op1=ALU.subtract).then_inc(done, 1)

            def add_rows(dst, src, b, base, done):
                dve.scalar_tensor_tensor(out=dst, in0=src, scalar=rstd[:, b:b + 1], in1=base, op0=ALU.mult, op1=ALU.add).then_inc(done, 1)

            def sum_groups(squares, blocks=slice(0, BLK)):
                dve.wait_ge(squares_ready, squares)
                dve.tensor_reduce(row_sum[:, blocks], sums[:, blocks], AX.X, ALU.add).then_inc(row_sums_ready, 1)

            def param(base, q):
                return par[:, q.c + base:q.c + base + 1] if q.i is None else par[:, bass.ds(q.i * q.k + (q.c + base), 1)]

            dve.wait_ge(par_turned, 1)
            dve.tensor_copy(par[:, 0:DC], ps[:, 2, 0:DC]).then_inc(par_ready, 1)
            dve.wait_ge(par_ready, 1)
            for c in range(DC):
                dve.wait_ge(turned_hi, c + 1)
                scaled_low(xg_lo[:, c], ps[:, 4 + c % 4], param(C_MIXPRE, At(c)), xg_hi[:, c], turned_split)
                if c in FIRST_SPLITS:
                    split(At(FIRST_SPLITS.index(c)))
            for k in range(2):
                step(At(U_A + k))
            dve.wait_ge(par_turned, 2)
            op(dve.tensor_copy(par[:, DC:C_CFB], ps[:, 5, DC:C_CFB]))
            dve.tensor_copy(par[:, C_CFB:C_ALL], ps[:, 6, 0:C_ALL - C_CFB]).then_inc(par_ready, 1)
            dve.wait_ge(par_ready, 2)
            dve.wait_ge(consts_ready, 3 + PPAD)
            token_factors(1)
            diagonals()
            for k in range(2, 4):
                step(At(U_A + k))
            factors_spread(1, 7, r_bc)

            op(dve.memset(a_conv[:, :, 0:PAD], 0.0))
            op(dve.memset(acc[:], 0.0))
            op.settle()

            def conv_taps(c, first, last):
                chunk = lambda k: flat(a_conv[:, bass.ds(c, 1), k:k + TOK])
                both = (conv_acc[:], sq[:, 1])
                for k in range(first, last):
                    weight = par[:, bass.ds(c + (C_CAW + k * HC), 1)]
                    op.settle(but=1 if k > 0 else 0)
                    if k == 0:
                        op(dve.tensor_scalar(both[0], chunk(0), weight, par[:, bass.ds(c + C_CAB, 1)], ALU.mult, ALU.add))
                    elif k == 1:
                        op(dve.tensor_scalar(both[1], chunk(1), weight, None, ALU.mult))
                    else:
                        op(dve.scalar_tensor_tensor(out=both[k % 2], in0=chunk(k), scalar=weight, in1=both[k % 2],
                                                    op0=ALU.mult, op1=ALU.add))
                if last == CONV_W:
                    op.settle()
                    op(dve.tensor_tensor(chunk(PAD), both[0], both[1], ALU.add))
                    op.settle()
                    op(dve.tensor_tensor(acc[:], acc[:], chunk(PAD), ALU.add))

            def glu_product(dst, t, sigmoids):
                scale_tile(tmp[:], t)
                dve.wait_ge(tiles_taken, (t + 1).value())
                dve.wait_ge(sigmoid_ready, sigmoids.value())
                op(dve.tensor_tensor(dst, tmp[:], sig[:], ALU.mult))

            def glu_chunks(i, js):
                for j in js:
                    taps = ((7, 13), (13, 19), (19, 26), (26, CONV_W)) if j == 1 else ((0, 0), (0, 0), (0, 0), (0, 7))
                    straight = isinstance(i, int)
                    at = lambda first, k: At(first + i * k) if straight else At(first, i, k)
                    u, t = at(U_A + 4 * j, 8), at(T_A + 2 * j, 4)
                    if straight and j == 0:
                        scale_tile(scaled[:], t)
                    else:
                        step(u)
                        conv_taps(i, *taps[0])
                        step(u + 1)
                        scale_tile(scaled[:], t)
                        conv_taps(i, *taps[1])
                        step(u + 2)
                        conv_taps(i, *taps[2])
                        step(u + 3)
                    glu_product(flat(a_conv[:, bass.ds(i * 2 + j, 1), PAD:]), t + 1, at(G_A + j + 1, 2))
                    conv_taps(i, *taps[3])

            glu_chunks(0, (0, 1))
            per = 2 + CONV_W + 2
            with dve.Fori(1, HC // 2) as i:
                op.enter(i, per, start=1)
                glu_chunks(i, (0, 1))
            op.leave(HC // 2, per, start=1)

            op(dve.memset(u_pool[:, 0:PPAD], 0.0))

            def pooled_low(c):
                dve.wait_ge(pooled_hi_ready, c + 1)
                low(pooled_lo[:, c], pool_f[:], pooled_hi[:, c], pooled_ready)

            TAPS_B = (0, 6, 12, 17, 22, 25, 28, 30, CONV_W)
            for c in range(HC):
                w = WINDOWS[c // 2]
                step(At(U_B + 2 * c))
                if c > 0:
                    pooled_low(c - 1)
                conv_taps(HC // 2, TAPS_B[c], TAPS_B[c + 1])
                step(At(U_B + 2 * c + 1))
                scale_tile(u_pool[:, PPAD:], At(T_B + c))
                dve.wait_ge(tiles_taken, T_B + c + 1)
                have, s = 1, u_pool
                while have < w:
                    dst = s_pool[:, have.bit_length() % 2]
                    op.settle()
                    op(dve.tensor_tensor(dst[:, 2 * have - 1:], s[:, 2 * have - 1:], s[:, have - 1:PPAD + TOK - have], ALU.add))
                    s, have = dst, 2 * have
                op.settle()
                op(dve.tensor_tensor(pool_f[:, 0:w - 1], s[:, PPAD:PPAD + w - 1], inv_count[:, 0:w - 1], ALU.mult))
                op.settle()
                op(dve.tensor_tensor(pool_f[:, 0:w - 1], pool_f[:, 0:w - 1], u_pool[:, PPAD:PPAD + w - 1], ALU.subtract))
                dve.scalar_tensor_tensor(out=pool_f[:, w - 1:], in0=s[:, PPAD + w - 1:], scalar=1.0 / w,
                                         in1=u_pool[:, PPAD + w - 1:], op0=ALU.mult, op1=ALU.subtract).then_inc(pool_f_ready, 1)
                dve.wait_ge(pool_f_ready, c + 1)

            def gated(dst, t, sigmoids, done):
                dve.wait_ge(sigmoid_ready, sigmoids.value())
                dve.tensor_tensor(dst, ps[:, t.slot(4)], sig[:], ALU.mult).then_inc(done, 1)

            def m1_taps(j):
                return ((8 * j, 8 * j + 3), (8 * j + 3, 8 * j + 5), (8 * j + 5, min(8 * j + 8, CONV_W)))

            step(At(U_M1 - 2))
            pooled_low(HC - 1)
            step(At(U_M1 - 1))
            scale_tile(scaled[:], At(T_M1))
            for n in range(2):
                for c in range(4 * n, 4 * n + 4):
                    dve.wait_ge(mixed_hi_ready, c + 1)
                    scaled_low(mixed_lo[:, c], ps[:, MAP_BANKS[c]], param(C_PSC, At(c)), mixed_hi[:, c], mixed_ready)
                step(At(U_M1 + n))
            step(At(U_M1 + 2))
            gated(merged[:, 0], At(T_M1 + 1), At(G_M1 + 1), tiles_taken)
            conv_taps(HC // 2 + 1, 0, 8)
            for j in range(1, 4):
                u, t, taps = At(U_M1 + 3 * j), At(T_M1 + 2 * j), m1_taps(j)
                step(u)
                conv_taps(HC // 2 + 1, *taps[0])
                step(u + 1)
                scale_tile(scaled[:], t)
                conv_taps(HC // 2 + 1, *taps[1])
                step(u + 2)
                gated(merged[:, j], t + 1, At(G_M1 + j + 1), tiles_taken)
                conv_taps(HC // 2 + 1, *taps[2])
            per = CONV_W + 2
            with dve.Fori(1, 3) as i:
                op.enter(i, per, start=1)
                for j in range(4):
                    c, taps = i + (HC // 2 + 1), m1_taps(j)
                    u, t = At(U_M1 + 3 * j, i, 12), At(T_M1 + 2 * j, i, 8)
                    step(u)
                    conv_taps(c, *taps[0])
                    step(u + 1)
                    scale_tile(scaled[:], t)
                    conv_taps(c, *taps[1])
                    step(u + 2)
                    gated(flat(merged[:, bass.ds(i * 4 + j, 1)]), t + 1, At(G_M1 + j + 1, i, 4), tiles_taken)
                    conv_taps(c, *taps[2])
            op.leave(3, per, start=1)
            op.settle()
            dve.tensor_scalar(acc[:], acc[:], 1.0 / H, None, ALU.mult).then_inc(mean_sum_ready, 1)
            def ln_scale(c):
                dve.scalar_tensor_tensor(out=a_conv[:, c, PAD:], in0=a_conv[:, c, PAD:], scalar=param(C_LNG, At(c)),
                                         in1=acc[:], op0=ALU.mult, op1=ALU.mult).then_inc(ln_scaled, 1)

            for j in range(4):
                u, t = At(U_M1 + 36 + 3 * j), At(T_M1 + 24 + 2 * j)
                step(u)
                if j == 3:
                    factors_spread(3, 7, acc)
                    for c in range(4):
                        ln_scale(c)
                step(u + 1)
                scale_tile(scaled[:], t)
                if j == 0:
                    dve.wait_ge(spread_done, 2)
                    op(dve.tensor_copy(tmp[:], ps[:, 7]))
                    op(dve.memset(acc[:], 0.0))
                    op.settle()
                step(u + 2)
                gated(merged[:, 12 + j], t + 1, At(G_M1 + 12 + j + 1), tiles_taken)
                if j < 2:
                    for c in range(4 * j, 4 * j + 4):
                        dve.tensor_tensor(a_conv[:, c, PAD:], a_conv[:, c, PAD:], tmp[:], ALU.subtract).then_inc(centred, 1)
                    for c in range(4 * j, 4 * j + 4):
                        dve.wait_ge(squares_ready, c + 1)
                        if c > 0:
                            dve.wait_ge(squares_added, c)
                        dve.tensor_tensor(acc[:], acc[:], sq[:, c % 2], ALU.add).then_inc(squares_added, 1)
                elif j == 2:
                    token_factors(2)
                    diagonals()
                else:
                    for c in range(4, HC):
                        ln_scale(c)

            def conv_branch(u, t, m, sigmoids, within_gate=None, ahead_of_branch=None):
                step(u)
                if within_gate:
                    within_gate()
                step(u + 1)
                scale_tile(scaled[:], t)
                if ahead_of_branch:
                    ahead_of_branch()
                step(u + 2)
                gated(tmp[:], t + 1, sigmoids, tiles_taken)
                dve.wait_ge(tiles_taken, (t + 2).value())
                dve.tensor_tensor(m, m, tmp[:], ALU.add).then_inc(merged_ready, 1)

            def conv_branch_low():
                for c in range(HC):
                    dve.wait_ge(a_hi_ready, c + 1)
                    low(a_lo[:, c], a_conv[:, c, PAD:], a_hi[:, c], a_ready)

            def merged_low(chunks):
                for c in chunks:
                    dve.wait_ge(merged_hi_ready, c + 1)
                    low(xg_lo[:, c], merged[:, c], xg_hi[:, c], merged_split)

            conv_branch(At(U_M2), At(T_M2), merged[:, 0], At(G_M2 + 1), within_gate=conv_branch_low)
            for m in range(1, 4):
                conv_branch(At(U_M2 + 3 * m), At(T_M2 + 2 * m), merged[:, m], At(G_M2 + m + 1))
            with dve.Fori(1, DC // 4 - 1) as i:
                for j in range(4):
                    conv_branch(At(U_M2 + 3 * j, i, 12), At(T_M2 + 2 * j, i, 8), flat(merged[:, bass.ds(i * 4 + j, 1)]),
                                At(G_M2 + j + 1, i, 4))
            for m in range(DC - 4, DC):
                conv_branch(At(U_M2 + 3 * m), At(T_M2 + 2 * m), merged[:, m], At(G_M2 + m + 1),
                            ahead_of_branch=(lambda: merged_low(range(EARLY))) if m == DC - 1 else None)
            merged_low(range(EARLY, DC))

            dve.wait_ge(gain_o_in, 16)
            def with_gain_o(n, b):
                dve.wait_ge(squares_ready, Q_O + 4 * n + b + 1)
                dve.tensor_tensor(og[:, n, b], ps[:, 4 * ((n + 1) % 2) + b], gain_o[:, n], ALU.mult).then_inc(tiles_taken, 1)

            for n in range(NG):
                for v in range(DC // 2 - (2 if n == NG - 1 else 0)):
                    step(At(U_O + 8 * n + v))
                for b in range(BLK - (2 if n == NG - 1 else 0)):
                    with_gain_o(n, b)
            last = BLK - 1
            sum_groups(Q_O + DC - 1, slice(0, last))
            with_gain_o(NG - 1, last - 1)
            dve.wait_ge(x_back, 16 * NG)
            dve.wait_ge(tiles_taken, T_F - 1)
            token_factors(3, slice(0, last))

            def x2_group(n):
                for b in range(BLK):
                    add_rows(x2[:, n, b], og[:, n, b], b, x2[:, n, b], x2_ready)

            for b in range(BLK):
                if b == last:
                    sum_groups(Q_O + DC, slice(last, BLK))
                    token_factors(4, slice(last, BLK))
                add_rows(x2[:, 0, b], og[:, 0, b], b, x2[:, 0, b], x2_ready)
            with_gain_o(NG - 1, last)
            for c in range(DC):
                dve.wait_ge(turned_hi, DC + c + 1)
                scaled_low(xg_lo[:, c], ps[:, 4 + c % 4], param(C_FFNPRE, At(c)), xg_hi[:, c], turned_split)
                if c % 4 == 1 and c < 12:
                    if c == 9:
                        dve.wait_ge(tiles_taken, T_F)
                    x2_group(c // 4 + 1)
                if c in (3, 5):
                    step(At(U_F - 2 + (c - 3) // 2))
                if c == 11:
                    step(At(U_F))
                    step(At(U_F + 1))
            token_factors(5)
            diagonals()
            for k in range(2, 4):
                step(At(U_F + k))
            factors_spread(4, 7, r_bc)

            op(dve.memset(up_gate[:, 0:2], 0.0))
            op(dve.memset(up_val[:, 0:2], 0.0))

            def up(u, t, q, half, first=False):
                def last_taps(dst, src, c, j, tally):
                    dve.wait_ge(first_tap_ready, At(2 * (q.c + c) + j + 1, q.i, 2 * q.k).value())
                    op(dve.scalar_tensor_tensor(out=dst[:], in0=src[:, 1:1 + TOK], scalar=param(C_CFW + 2 * FC + j * FC, q + c),
                                                in1=dst[:], op0=ALU.mult, op1=ALU.add))
                    op.settle()
                    tally(dve.scalar_tensor_tensor(out=dst[:], in0=src[:, 2:2 + TOK], scalar=param(C_CFW + 4 * FC + j * FC, q + c),
                                                   in1=dst[:], op0=ALU.mult, op1=ALU.add))

                def product(c):
                    last_taps(val_c, up_val, c, 1, op)
                    op.settle()
                    dve.wait_ge(gelu_ready, (q + (c + 1)).value())
                    dve.tensor_tensor(ff_prod[:], gelu_g[:], val_c[:], ALU.mult).then_inc(ff_ready, 1)

                def product_low(c):
                    dve.wait_ge(g_hi_ready, (q + (c + 1)).value())
                    low(g_lo[:, half, c], ff_prod[:], g_hi[:, half, c], g_ready)

                def gate_taps(c):
                    last_taps(gate_c, up_gate, c, 0, lambda ins: ins.then_inc(gate_conv_ready, 1))

                for c in range(GRP):
                    take = lambda dst, w: scale_tile(dst[:, 2:], t + w, bank=w)
                    if first and c == 0:
                        take(up_gate, 0)
                        gate_taps(c)
                        take(up_val, 1)
                        continue
                    step(u + 4 * c)
                    if c > 0:
                        product(c - 1)
                    step(u + (4 * c + 1))
                    if c > 0:
                        product_low(c - 1)
                    take(up_gate, 2 * c)
                    step(u + (4 * c + 2))
                    gate_taps(c)
                    step(u + (4 * c + 3))
                    take(up_val, 2 * c + 1)
                product(GRP - 1)
                product_low(GRP - 1)

            def down_add(n, b):
                dve.tensor_tensor(f_acc[:, n, b], f_acc[:, n, b], ps[:, 4 * (n % 2) + b], ALU.add).then_inc(tiles_taken, 1)

            def down(u, t):
                for n in range(NG):
                    for v in range(2):
                        step(u + (2 * n + v))
                    for b in range(BLK):
                        down_add(n, b)

            def with_gain_f(n, b):
                dve.wait_ge(squares_ready, Q_F + 4 * n + b + 1)
                op(dve.tensor_tensor(f_acc[:, n, b], f_acc[:, n, b], gain_f[:, n], ALU.mult))

            up(At(F_UP(0)), At(FT_UP(0)), At(0), 0, first=True)
            dve.wait_ge(f_zero, 1)
            per = 2 * GRP * 3
            with dve.Fori(0, (NGRP - 1) // 2) as i:
                op.enter(i, per)
                for s in range(2):
                    up(At(F_UP(1 + s), i, 48), At(FT_UP(1 + s), i, 48), At(GRP * (1 + s), i, 2 * GRP), 1 - s)
                    down(At(F_DOWN(s), i, 48), At(FT_DOWN(s), i, 48))
            op.leave((NGRP - 1) // 2, per)
            for n in range(NG):
                by_block = n == NG - 1
                for v in range(0 if by_block else 2):
                    step(At(F_DOWN(NGRP - 1) + 2 * n + v))
                    if n == 0 and v == 0:
                        for k in range(PLEC):
                            dve.wait_ge(p_hi_ready, k + 1)
                            low(p_lo[:, k], ps[:, 6 + k], p_hi[:, k], p_ready)
                        dve.wait_ge(gain_f_in, 16)
                for b in range(BLK):
                    if by_block and b < BLK - 1:
                        dve.wait_ge(blocks_done, 3 + b + 1)
                    elif by_block:
                        dve.wait_ge(units_done, U_L)
                    down_add(n, b)
                    if by_block and b > 0:
                        with_gain_f(n, b - 1)
                if not by_block:
                    for b in range(BLK):
                        with_gain_f(n, b)
            sum_groups(Q_F + DC)
            with_gain_f(NG - 1, BLK - 1)
            op.settle()
            token_factors(6)

            def x3_group(n):
                dve.wait_ge(x2_in[n], 16)
                for b in range(BLK):
                    add_rows(x3[:, n, b], f_acc[:, n, b], b, x3[:, n, b], x3_ready)

            x3_group(0)
            for k in (2, 1):
                step(At(U_L - k))
            x3_group(1)
            for k in range(3):
                step(At(U_L + k))
            for c in range(DC):
                dve.wait_ge(turned_hi, 2 * DC + c + 1)
                low(x3_lo[:, c], ps[:, 4 + c % 4], x3_hi[:, c], turned_split)
                if c == 1:
                    step(At(U_L + 3))
                if c in (3, 7):
                    x3_group(2 + c // 4)
                if c % 4 == 3 and c > 4:
                    step(At(U_G + c // 4 - 1))

            def gate_p(n, b):
                dve.wait_ge(sigmoid_ready, G_G + 4 * n + b + 1)
                dve.tensor_tensor(e_buf[:, n, b], e_buf[:, n, b], (sig, scaled)[b % 2][:], ALU.mult).then_inc(tiles_taken, 1)

            def with_gain_e(n, b):
                dve.wait_ge(squares_ready, Q_E + 4 * n + b + 1)
                op(dve.tensor_tensor(e_buf[:, n, b], e_buf[:, n, b], gain_e[:, n], ALU.mult))

            for n in range(NG):
                for v in range(3 if n == 0 else 0, DC // 2):
                    if U_G + 8 * n + v + SLOTS < U_END:
                        step(At(U_G + 8 * n + v))
                if n == NG - 1:
                    continue
                for b in range(BLK):
                    gate_p(n, b)
                if n == 0:
                    dve.wait_ge(gain_e_in, 16)
                for b in range(BLK):
                    with_gain_e(n, b)
            n = NG - 1

            def finish(b, groups=range(NG)):
                for m in groups:
                    add_rows(e_buf[:, m, b], e_buf[:, m, b], b, x3[:, m, b], y_ready)

            first, second = range(NG // 2), range(NG // 2, NG)
            for b in range(2):
                gate_p(n, b)
                with_gain_e(n, b)
            sum_groups(Q_E + 4 * n + 2, slice(0, 2))
            token_factors(7, slice(0, 2))
            finish(0)
            gate_p(n, 2)
            finish(1, first)
            sum_groups(Q_E + 4 * n + 3, slice(2, 3))
            finish(1, second)
            with_gain_e(n, 2)
            token_factors(8, slice(2, 3))
            gate_p(n, 3)
            finish(2, first)
            sum_groups(Q_E + 4 * n + 4, slice(3, 4))
            finish(2, second)
            with_gain_e(n, 3)
            token_factors(9, slice(3, 4))
            finish(3)


NAMES = ["x", "p", "mix_pre_g", "w_in", "conv_a_w", "conv_a_b", "ln_a_g", "ln_a_b", "w_a_out", "pool_w", "pool_scale",
         "w_b_out", "w_o", "mix_post_g", "ffn_pre_g", "w_up", "conv_f_w", "conv_f_b", "w_down", "ffn_post_g", "w_ple",
         "w_ple_gate", "ple_post_g"]


def kernel(**inputs):
    import concourse.bacc as bacc
    from concourse.bass_utils import run_bass_kernel_spmd

    nc = bacc.Bacc("TRN2", target_bir_lowering=False, num_devices=1)
    arrays, args = {}, []
    for name in NAMES:
        a = np.ascontiguousarray(inputs[name])
        arrays[f"in_{name}"] = a
        args.append(nc.dram_tensor(f"in_{name}", a.shape, mybir.dt.from_np(a.dtype), kind="ExternalInput").ap())
    out = nc.dram_tensor("out_0", (1, TOK, D), F32, kind="ExternalOutput").ap()
    build(nc, *args, out)
    r = run_bass_kernel_spmd(nc, [arrays], core_ids=[0])
    return r.results[0]["out_0"]
```
